# Optimizing a Trainium2 kernel written in Bass

```python
import jax, jax.numpy as jnp
from jax import lax
import numpy as np

D_MODEL = 2048
BATCH = 1
SEQ = 256
DEPTH = 1

N_ATTN_HEADS = 8
HEAD_DIM = 128
D_ATTN = N_ATTN_HEADS * HEAD_DIM
D_CONV = D_MODEL - D_ATTN
D_MIX = D_ATTN + D_CONV
D_IN = 3 * D_ATTN + 2 * D_CONV
DILATED_BRANCHES = ((128, 1), (512, 4), (2048, 16))
BLK = 128
CONV_WIDTH = 31
D_FF = ((-(-8 * D_MODEL // 3) + 255) // 256) * 256
D_PLE = 256
EPS = 1e-6

kernel_name = "hymba_dilated_attn_conformer_conv_hybrid"

def rmsnorm(x, g):
    xf = x.astype(jnp.float32)
    y = xf * lax.rsqrt(jnp.mean(xf * xf, axis=-1, keepdims=True) + EPS)
    return (y * g.astype(jnp.float32)).astype(x.dtype)

def layernorm(x, g, b):
    xf = x.astype(jnp.float32)
    mu = jnp.mean(xf, axis=-1, keepdims=True)
    var = jnp.mean(jnp.square(xf - mu), axis=-1, keepdims=True)
    y = (xf - mu) * lax.rsqrt(var + EPS)
    return (y * g.astype(jnp.float32) + b.astype(jnp.float32)).astype(x.dtype)

def dilated_branch(q, k, v, window, dilation):
    B, S, H, Dh = q.shape
    span = dilation * BLK
    L = -(-S // span) * span
    nb = L // span
    pad = ((0, 0), (0, L - S), (0, 0), (0, 0))

    def blocks(a):
        return jnp.pad(a, pad).reshape(B, nb, BLK, dilation, H, Dh)

    def with_prev(a):
        prev = jnp.pad(a, ((0, 0), (1, 0), (0, 0), (0, 0), (0, 0), (0, 0)))[:, :-1]
        return jnp.concatenate([prev, a], axis=2)

    qb = blocks(q)
    kk = with_prev(blocks(k))
    vv = with_prev(blocks(v))
    s = jnp.einsum('bnqrhd,bnkrhd->bnrhqk', qb, kk).astype(jnp.float32) * (Dh ** -0.5)
    qi = jnp.arange(BLK)[:, None]
    kj = jnp.arange(2 * BLK)[None, :]
    dist = qi + BLK - kj
    band = (dist >= 0) & (dist <= window // dilation)
    first = (jnp.arange(nb)[:, None, None] > 0) | (kj[None] >= BLK)
    mask = band[None] & first
    s = jnp.where(mask[None, :, None, None], s, -jnp.inf)
    m = jnp.max(s, axis=-1, keepdims=True)
    e = jnp.exp(s - m)
    den = jnp.sum(e, axis=-1, keepdims=True)
    o = jnp.einsum('bnrhqk,bnkrhd->bnqrhd', (e / den).astype(v.dtype), vv)
    o = o.reshape(B, L, H, Dh)[:, :S]
    lse = (m + jnp.log(den))[..., 0]
    lse = lse.transpose(0, 1, 4, 2, 3).reshape(B, L, H)[:, :S]
    return o, lse

def dilated_attention(q, k, v):
    outs, lses = [], []
    for window, dilation in DILATED_BRANCHES:
        o, lse = dilated_branch(q, k, v, window, dilation)
        outs.append(o)
        lses.append(lse)
    w = jax.nn.softmax(jnp.stack(lses, axis=0), axis=0)
    o = jnp.sum(w[..., None] * jnp.stack(outs, axis=0).astype(jnp.float32), axis=0)
    return o.astype(q.dtype)

def conformer_conv(cv, cg, w_dw, b_dw, g_ln, b_ln):
    u = cv * jax.nn.sigmoid(cg)
    u = lax.conv_general_dilated(u, w_dw.astype(u.dtype), window_strides=(1,),
                                 padding=[(CONV_WIDTH - 1, 0)],
                                 dimension_numbers=('NWC', 'WIO', 'NWC'),
                                 feature_group_count=D_CONV) + b_dw
    return jax.nn.silu(layernorm(u, g_ln, b_ln))

def setup_inputs(seed: int = 0) -> dict:
    key = jax.random.key(seed)
    ks = jax.random.split(key, 20)

    def nrm(k, shape, scale):
        return jax.random.normal(k, shape, jnp.float32) * scale

    def gain(k, n):
        return 1.0 + 0.02 * jax.random.normal(k, (DEPTH, n), jnp.float32)

    return {
        "x": nrm(ks[0], (BATCH, SEQ, D_MODEL), 1.0),
        "p": nrm(ks[1], (DEPTH, BATCH, SEQ, D_PLE), 1.0),
        "g_mix": gain(ks[2], D_MODEL),
        "w_in": nrm(ks[3], (DEPTH, D_MODEL, D_IN), D_MODEL ** -0.5),
        "w_dw": nrm(ks[4], (DEPTH, CONV_WIDTH, 1, D_CONV), CONV_WIDTH ** -0.5),
        "b_dw": nrm(ks[5], (DEPTH, D_CONV), 0.02),
        "g_conv_ln": gain(ks[6], D_CONV),
        "b_conv_ln": nrm(ks[7], (DEPTH, D_CONV), 0.02),
        "w_out": nrm(ks[8], (DEPTH, D_MIX, D_MODEL), D_MIX ** -0.5),
        "g_ffn": gain(ks[9], D_MODEL),
        "w_gate": nrm(ks[10], (DEPTH, D_MODEL, D_FF), D_MODEL ** -0.5),
        "w_up": nrm(ks[11], (DEPTH, D_MODEL, D_FF), D_MODEL ** -0.5),
        "w_down": nrm(ks[12], (DEPTH, D_FF, D_MODEL), D_FF ** -0.5),
        "g_ple": gain(ks[13], D_MODEL),
        "w_pgate": nrm(ks[14], (DEPTH, D_MODEL, D_MODEL), D_MODEL ** -0.5),
        "b_pgate": nrm(ks[15], (DEPTH, D_MODEL), 0.02),
        "w_ple": nrm(ks[16], (DEPTH, D_PLE, D_MODEL), D_PLE ** -0.5),
        "g_final": 1.0 + 0.02 * jax.random.normal(ks[17], (D_MODEL,), jnp.float32),
    }

def reference(x, p, g_mix, w_in, w_dw, b_dw, g_conv_ln, b_conv_ln, w_out, g_ffn,
              w_gate, w_up, w_down, g_ple, w_pgate, b_pgate, w_ple, g_final):
    B, S, _ = x.shape
    h = x
    for i in range(DEPTH):
        a = rmsnorm(h, g_mix[i])
        z = a @ w_in[i]
        q, k, v, cv, cg = jnp.split(
            z, [D_ATTN, 2 * D_ATTN, 3 * D_ATTN, 3 * D_ATTN + D_CONV], axis=-1)
        hd = (B, S, N_ATTN_HEADS, HEAD_DIM)
        o_attn = dilated_attention(q.reshape(hd), k.reshape(hd), v.reshape(hd)).reshape(B, S, D_ATTN)
        o_conv = conformer_conv(cv, cg, w_dw[i], b_dw[i], g_conv_ln[i], b_conv_ln[i])
        h = h + jnp.concatenate([o_attn, o_conv], axis=-1) @ w_out[i]
        f = rmsnorm(h, g_ffn[i])
        h = h + (jax.nn.silu(f @ w_gate[i]) * (f @ w_up[i])) @ w_down[i]
        gte = jax.nn.sigmoid(rmsnorm(h, g_ple[i]) @ w_pgate[i] + b_pgate[i])
        h = h + (p[i] @ w_ple[i]) * gte
    return rmsnorm(h, g_final)


_drawn_inputs = setup_inputs


def setup_inputs(seed=0):
    import zlib

    import numpy as np

    out = dict(_drawn_inputs(seed))
    spreads = {}
    factors = {'g_mix': 5.547,
     'b_dw': 10.19,
     'g_conv_ln': 18.975,
     'b_conv_ln': 19.963,
     'g_ffn': 4.358,
     'g_ple': 64.0,
     'b_pgate': 64.0,
     'g_final': 8.0}
    for name, (base, spread) in spreads.items():
        noise = np.random.default_rng([zlib.crc32(name.encode()), seed]).standard_normal(out[name].shape)
        drawn = base * np.exp(spread * noise) if base else spread * noise
        out[name] = __import__('jax').numpy.asarray(drawn.astype(out[name].dtype))
    for name, factor in factors.items():
        out[name] = (out[name] * factor).astype(out[name].dtype)
    return out
```

```python
import concourse.bass as bass
from concourse import mybir
from contextlib import ExitStack

F32 = mybir.dt.float32
F32R = mybir.dt.float32r
I32 = mybir.dt.int32
ALU = mybir.AluOpType
ACT = mybir.ActivationFunctionType
AX = mybir.AxisListType

P = 128
T = 256
TT = T // P
D = 2048
KC = D // P
NP = 512
HEADS, DH = 8, 128
D_ATTN = HEADS * DH
D_CONV = D - D_ATTN
CC = D_CONV // P
TAPS = 31
PAD = TAPS - 1
D_FF = 5632
FP = D_FF // NP
D_PLE = 256
EPS = 1e-6
SCALE = float(DH) ** -0.5
NEG = -1e30

IN0 = 0
IN_PANELS = ["cv0", "cg0", "cv1", "cg1", "q0", "k0", "v0", "q1", "k1", "v1"]
IN_COLUMN = {"q": 0, "k": D_ATTN, "v": 2 * D_ATTN, "cv": 3 * D_ATTN, "cg": 3 * D_ATTN + D_CONV}
WO_A = IN0 + 8 * len(IN_PANELS)
WO_C = WO_A + 8
WO_B = WO_C + 16
FFN0 = WO_B + 8
LOOP0 = FFN0 + 16
LOOPS = FP - 1
PER_LOOP = 24
PLE0 = LOOP0 + PER_LOOP * LOOPS
DOWN0 = PLE0 + 4
PG0 = DOWN0 + 8
END = PG0 + 32
RAW = 4
SLOTS = 4
AHEAD = SLOTS
POOL_UNTIL = FFN0

Q_WO_A, Q_WO_C, Q_WO_B = 10, 14, 18
Q_DOWN = 22
Q_DOWN_LAST = Q_DOWN + 4 * LOOPS
Q_PG = Q_DOWN_LAST + 4

SCORES_AT = {h: (49 + 2 * h if h < 4 else 73 + 2 * (h - 4)) for h in range(HEADS)}
TURN_AT = {h: SCORES_AT[h] + 3 for h in range(HEADS)}
VALUES_AT = {h: (58 + 2 * h if h < 4 else 82 + 2 * (h - 4)) for h in range(HEADS)}

CONV_STEPS = [(17, 47), (47, 77)]
CONV_OPS = 4 * TAPS
MEAN_AT, VAR_AT, SPREAD_AT = 78, 81, 83

G_MIX, G_FFN, G_PLE, B_DW, G_LN, B_LN, N_PAR = 0, 16, 32, 48, 56, 64, 72


def lo_count(m, it=0):
    if m < POOL_UNTIL:
        return (m // 2 + 1, None) if m % 2 == 0 else (None, m // 2 + 1)
    return POOL_UNTIL // 2 + m - POOL_UNTIL + 1 + PER_LOOP * it, None


def hybrid_decoder_layer(nc, x, p, g_mix, w_in, w_dw, b_dw, g_conv_ln, b_conv_ln, w_out, g_ffn,
                         w_gate, w_up, w_down, g_ple, w_pgate, b_pgate, w_ple, g_final, out):
    x_rows = x[0].rearrange("(t p) d -> p t d", p=P)
    out_rows = out[0].rearrange("(t p) d -> p t d", p=P)
    p_rows = p[0, 0].rearrange("(t p) d -> p t d", p=P)

    def by_rows(w):
        return w[0].rearrange("(k p) n -> p k n", p=P)

    w_in_v, w_out_v, w_gate_v, w_up_v = by_rows(w_in), by_rows(w_out), by_rows(w_gate), by_rows(w_up)
    w_down_v, w_pgate_v, w_ple_v = by_rows(w_down), by_rows(w_pgate), by_rows(w_ple)

    with ExitStack() as ctx:
        def sb(name, shape, dt=F32):
            return ctx.enter_context(nc.sbuf_tensor(name, shape, dt))

        def sem(name):
            return ctx.enter_context(nc.semaphore(name))

        w_raw = sb("w_raw", [P, RAW, 4, NP])
        w_hi = sb("w_hi", [P, SLOTS, 2, NP], F32R)
        w_lo = sb("w_lo", [P, SLOTS, 2, NP], F32R)
        nT_hi = sb("nT_hi", [P, KC, T], F32R)
        nT_lo = sb("nT_lo", [P, KC, T], F32R)
        oT_hi = sb("oT_hi", [P, KC, T], F32R)
        oT_lo = sb("oT_lo", [P, KC, T], F32R)
        pleT_hi = sb("pleT_hi", [P, 2, T], F32R)
        pleT_lo = sb("pleT_lo", [P, 2, T], F32R)
        h = sb("h", [P, TT, D])
        ident = sb("ident", [P, P])
        mean_w = sb("mean_w", [P, P])
        par = sb("par", [P, N_PAR])
        taps = sb("taps", [P, CC, 32])
        rb = sb("rb", [P, T])
        count = sb("count", [P, 384])
        mask = sb("mask", [P, 384])
        junk = sb("junk", [P, NP])
        sq = sb("sq", [P, 4, TT, 4])
        msq = sb("msq", [P, 5, TT])
        rstd = sb("rstd", [P, 5, TT])
        power = sb("power", [P, TT])
        top = sb("top", [P, HEADS, TT])
        ntop = sb("ntop", [P, HEADS, TT])
        den = sb("den", [P, HEADS, TT])
        rden = sb("rden", [P, HEADS, TT])
        arena = sb("arena", [P, 11504])

        def part(at, *shape):
            n = 1
            for s in shape:
                n *= s
            v = arena[:, at:at + n]
            return v.rearrange("p (a b) -> p a b", b=shape[-1]) if len(shape) == 2 else v

        qT, kT = part(0, 4, T), part(1024, 4, T)
        v_sb = part(2048, TT, D_ATTN)
        u = part(4096, CC, PAD + T)
        conv = part(6384, CC, T)
        masked = part(8432, 2, 384)
        prob = part(9200, 2, 384)
        probT = part(9968, 4, 384)
        gate_c = part(9968, 4, T)
        dist = part(8432, 384).bitcast(I32)
        dist4 = part(8816, 384).bitcast(I32)
        dist16 = part(9200, 384).bitcast(I32)
        branches = part(9584, 384)
        p_raw = part(6384, TT, D_PLE)
        taps_raw = part(6896, D_CONV)
        par_raw = part(7920, P)
        swish = part(0, TT, NP)
        act = part(1024, TT, NP)
        gate_p = part(0, TT, NP)
        pw = part(2048, TT, D)
        b_rows = part(6144, D)
        gf_rows = part(8192, D)

        ps = [ctx.enter_context(nc.psum_tensor(f"ps{i}", [P, NP], F32)) for i in range(8)]
        LOW = [(ps[0], ps[1]), (ps[2], ps[3])]
        HIGH = [(ps[4], ps[5]), (ps[6], ps[7])]

        def pair_of(q):
            return LOW[q % 2] if q < Q_DOWN else HIGH[q % 2]

        raw_ready = [sem(f"raw_ready{i}") for i in range(RAW)]
        x_loaded = [sem(f"x_loaded{i}") for i in range(4)]
        par_loaded, small_loaded, rows_loaded = sem("par_loaded"), sem("small_loaded"), sem("rows_loaded")
        out_stored = [sem("out_stored0"), sem("out_stored1")]
        hi_ready, lo_ready, lo_ready_pool = sem("hi_ready"), sem("lo_ready"), sem("lo_ready_pool")
        half_done = sem("half_done")
        panel_read = sem("panel_read")
        consts_ready, ident_ready, pad_ready, dist_ready = sem("consts_ready"), sem("ident_ready"), sem("pad_ready"), sem("dist_ready")
        par_turned, par_ready = sem("par_turned"), sem("par_ready")
        small_turned, taps_ready, pleT_hi_ready, pleT_ready = sem("small_turned"), sem("taps_ready"), sem("pleT_hi_ready"), sem("pleT_ready")
        mask_step = sem("mask_step")
        hT_done, nT_hi_ready, nT_ready = sem("hT_done"), sem("nT_hi_ready"), sem("nT_ready")
        sq_ready, sum_ready, msq_ready, rstd_ready = sem("sq_ready"), sem("sum_ready"), sem("msq_ready"), sem("rstd_ready")
        rb_spread, rb_ready = sem("rb_spread"), sem("rb_ready")
        gate_c_ready, u_ready = sem("gate_c_ready"), sem("u_ready")
        conv_step = sem("conv_step")
        mean_ready, centered, dev_squared, var_ready = sem("mean_ready"), sem("centered"), sem("dev_squared"), sem("var_ready")
        ln_spread, ln_scaled, ln_silu, convT_hi_ready, convT_ready = sem("ln_spread"), sem("ln_scaled"), sem("ln_silu"), sem("convT_hi_ready"), sem("convT_ready")
        scores_ready, masked_ready, ntop_ready, exp_ready = sem("scores_ready"), sem("masked_ready"), sem("ntop_ready"), sem("exp_ready")
        den_ready, rden_ready, prob_ready = sem("den_ready"), sem("rden_ready"), sem("prob_ready")
        probT_turned, probT_ready, o_done, oT_hi_ready, oT_ready = sem("probT_turned"), sem("probT_ready"), sem("o_done"), sem("oT_hi_ready"), sem("oT_ready")
        h_ready = sem("h_ready")
        swish_ready, act_ready, actT_turned, actT_hi_ready, actT_ready = sem("swish_ready"), sem("act_ready"), sem("actT_turned"), sem("actT_hi_ready"), sem("actT_ready")
        pw_ready, gate_in, gate_p_ready, gated = sem("pw_ready"), sem("gate_in"), sem("gate_p_ready"), sem("gated")
        hg_ready, y_ready = sem("hg_ready"), [sem("y_ready0"), sem("y_ready1")]

        block = ctx.enter_context(nc.Block())

        @block.sync
        def _(sp):
            def load(n, src, it=0, dst=None):
                if n >= RAW:
                    last = 2 * (n - RAW) + 1
                    if last < POOL_UNTIL:
                        sp.wait_ge(lo_ready, lo_count(last - 1)[0])
                        sp.wait_ge(lo_ready_pool, lo_count(last)[1])
                    else:
                        sp.wait_ge(lo_ready, lo_count(last, it)[0])
                sp.dma_start(w_raw[:, n % RAW] if dst is None else dst, src).then_inc(raw_ready[n % RAW], 16)

            for at, v, rows in ((G_MIX, g_mix, KC), (G_FFN, g_ffn, KC), (G_PLE, g_ple, KC),
                                (B_DW, b_dw, CC), (G_LN, g_conv_ln, CC), (B_LN, b_conv_ln, CC)):
                sp.dma_start(par_raw[at:at + rows, :], v[0].rearrange("(r c) -> r c", c=P)).then_inc(par_loaded, 16)
            n = 0
            for panel in IN_PANELS:
                column = IN_COLUMN[panel[:-1]] + NP * int(panel[-1])
                for k in range(4):
                    if n == 1:
                        sp.dma_start(taps_raw[0:TAPS, :], w_dw[0, :, 0, :]).then_inc(small_loaded, 16)
                        sp.dma_start(p_raw[:, :, :], p_rows).then_inc(small_loaded, 16)
                    if n < 4:
                        cols = slice(n * NP, (n + 1) * NP)
                        sp.dma_start(h[:, :, cols], x_rows[:, :, cols]).then_inc(x_loaded[n], 16)
                    load(n, w_in_v[:, 4 * k:4 * k + 4, column:column + NP])
                    n += 1
            for blocks in ((0,), (2, 3), (1,)):
                for c in range(4):
                    for k in blocks:
                        load(n, w_out_v[:, 4 * k:4 * k + 4, c * NP:(c + 1) * NP])
                        n += 1
            for w in (w_gate_v, w_up_v):
                for k in range(4):
                    load(n, w[:, 4 * k:4 * k + 4, 0:NP])
                    n += 1
            sp.wait_ge(convT_ready, 2)
            sp.wait_ge(oT_ready, HEADS)
            sp.dma_start(b_rows, b_pgate[0].partition_broadcast(P)).then_inc(rows_loaded, 16)
            sp.dma_start(gf_rows, g_final.partition_broadcast(P)).then_inc(rows_loaded, 16)
            with sp.Fori(0, LOOPS) as it:
                for i, w in enumerate((w_gate_v, w_up_v)):
                    for k in range(4):
                        load(n + 4 * i + k, w[:, 4 * k:4 * k + 4, bass.ds(it * NP + NP, NP)], it)
                for c in range(4):
                    load(n + 8 + c, w_down_v[:, bass.ds(it * 4, 4), c * NP:(c + 1) * NP], it)
            n = PLE0 // 2
            for c in range(2):
                load(n, w_ple_v[:, :, 2 * c * NP:2 * (c + 1) * NP],
                     dst=w_raw[:, n % RAW].rearrange("p (k f) n -> p k (f n)", f=2))
                n += 1
            for c in range(4):
                load(n, w_down_v[:, 4 * LOOPS:4 * LOOPS + 4, c * NP:(c + 1) * NP])
                n += 1
            for c in range(4):
                for k in range(4):
                    load(n, w_pgate_v[:, 4 * k:4 * k + 4, c * NP:(c + 1) * NP])
                    n += 1
            for t in range(TT):
                sp.wait_ge(y_ready[t], 1)
                sp.dma_start(out_rows[:, t], h[:, t]).then_inc(out_stored[t], 16)
            for t in range(TT):
                sp.wait_ge(out_stored[t], 16)

        @block.gpsimd
        def _(pool):
            nc.gpsimd.memset(ident[:, :], 0.0).then_inc(ident_ready, 1)
            nc.gpsimd.memset(mean_w[:, :], 1.0 / D_CONV).then_inc(consts_ready, 1)
            nc.gpsimd.memset(power[:, :], -0.5).then_inc(consts_ready, 1)
            pool.wait_ge(ident_ready, 1)
            nc.gpsimd.affine_select(out=ident[:, :], in_=ident[:, :], compare_op=ALU.not_equal, fill=1.0,
                                    base=0, pattern=[[-1, P]], channel_multiplier=1).then_inc(ident_ready, 1)
            nc.gpsimd.iota(dist[:, 0:P], pattern=[[-1, P]], base=0, channel_multiplier=1).then_inc(dist_ready, 1)
            nc.gpsimd.iota(dist[:, P:384], pattern=[[-1, T]], base=P, channel_multiplier=1).then_inc(dist_ready, 1)
            nc.gpsimd.memset(u[:, :, 0:PAD], 0.0).then_inc(pad_ready, 1)

            def root(norm, order):
                if order == 0:
                    pool.wait_ge(consts_ready, 2)
                pool.wait_ge(msq_ready, order + 1)
                nc.gpsimd.tensor_tensor(rstd[:, norm], msq[:, norm], power[:, :], ALU.pow).then_inc(rstd_ready, 1)

            def split_lo(m):
                pool.wait_ge(hi_ready, m + 1)
                if m >= SLOTS:
                    pool.wait_ge(half_done, m - SLOTS + 1)
                rows = slice(2 * (m % 2), 2 * (m % 2) + 2)
                nc.gpsimd.tensor_tensor(w_lo[:, m % SLOTS], w_raw[:, (m // 2) % RAW, rows],
                                        w_hi[:, m % SLOTS].bitcast(F32), ALU.subtract).then_inc(lo_ready_pool, 1)

            for m in range(1, POOL_UNTIL, 2):
                if m == AHEAD + 7:
                    root(0, 0)
                if m == AHEAD + VAR_AT:
                    root(4, 1)
                split_lo(m)
            root(1, 2)
            root(2, 3)
            pool.wait_ge(rows_loaded, 32)
            for c in range(3):
                pool.wait_ge(sq_ready, 8 * 3 + 2 * (c + 1))
                for t in range(TT):
                    cols = slice(c * NP, (c + 1) * NP)
                    nc.gpsimd.tensor_tensor(h[:, t, cols], h[:, t, cols], gf_rows[:, cols], ALU.mult).then_inc(hg_ready, 1)
            root(3, 4)

        @block.scalar
        def _(sc):
            def split_hi(m, it=0):
                sc.wait_ge(raw_ready[(m // 2) % RAW], 16 * (m // 2 // RAW + 1) + 48 * it)
                if m >= SLOTS:
                    sc.wait_ge(half_done, m - SLOTS + 1 + PER_LOOP * it)
                rows = slice(2 * (m % 2), 2 * (m % 2) + 2)
                nc.scalar.activation(w_hi[:, m % SLOTS], w_raw[:, (m // 2) % RAW, rows], ACT.Copy).then_inc(hi_ready, 1)

            squares = [0]

            def sum_squares(norm, c):
                for t in range(TT):
                    if squares[0]:
                        sc.wait_ge(sq_ready, squares[0])
                    nc.scalar.activation(junk[:, :], h[:, t, c * NP:(c + 1) * NP], ACT.Square,
                                         accum_out=sq[:, norm, t, c:c + 1]).then_inc(sq_ready, 1)
                    squares[0] += 1

            def gain_hi(norm, g_at, c, banks):
                sc.wait_ge(hT_done, 4 * norm + c + 1)
                for k in range(4):
                    ins = nc.scalar.activation(nT_hi[:, 4 * c + k], banks[k // 2][:, (k % 2) * T:(k % 2 + 1) * T],
                                               ACT.Identity, scale=par[:, g_at + 4 * c + k:g_at + 4 * c + k + 1])
                ins.then_inc(nT_hi_ready, 1)

            def exps(hd):
                sc.wait_ge(ntop_ready, hd + 1)
                if hd >= 2:
                    sc.wait_ge(probT_turned, hd - 1)
                for lo, hi, t in ((0, P, 0), (P, 384, 1)):
                    ins = nc.scalar.activation(prob[:, hd % 2, lo:hi], masked[:, hd % 2, lo:hi], ACT.Exp,
                                               scale=SCALE, bias=ntop[:, hd, t:t + 1])
                ins.then_inc(exp_ready, 1)

            sc.wait_ge(par_ready, 1)
            gain_hi(0, G_MIX, 0, HIGH[0])
            for m in range(AHEAD):
                split_hi(m)

            def step(m):
                for c in range(4):
                    if c and m == 2 * c - 1:
                        gain_hi(0, G_MIX, c, HIGH[c % 2])
                    if m == 2 * c:
                        sum_squares(0, c)
                if m == 4:
                    sc.wait_ge(small_turned, 1)
                    nc.scalar.activation(pleT_hi[:, :, :], ps[3][:, :].rearrange("p (k t) -> p k t", k=2),
                                         ACT.Copy).then_inc(pleT_hi_ready, 1)
                for g in range(2):
                    if m == 16 * (g + 1):
                        sc.wait_ge(panel_read, 2 * g + 2)
                        nc.scalar.activation(gate_c[:, :, :], gate_c[:, :, :], ACT.Sigmoid).then_inc(gate_c_ready, 1)
                for hd in range(HEADS):
                    if m == SCORES_AT[hd]:
                        exps(hd)
                    if m == TURN_AT[hd]:
                        sc.wait_ge(probT_turned, hd + 1)
                        if hd >= 4:
                            sc.wait_ge(o_done, hd - 3)
                        nc.scalar.activation(probT[:, hd % 4], ps[6][:, 0:384], ACT.Copy).then_inc(probT_ready, 1)
                    if m == VALUES_AT[hd]:
                        sc.wait_ge(o_done, hd + 1)
                        nc.scalar.activation(oT_hi[:, hd], ps[7][:, 0:T], ACT.Copy).then_inc(oT_hi_ready, 1)
                if m == MEAN_AT + 1:
                    for i in range(4):
                        sc.wait_ge(centered, i + 1)
                        nc.scalar.activation(u[:, 2 * i:2 * i + 2, 0:T], conv[:, 2 * i:2 * i + 2],
                                             ACT.Square).then_inc(dev_squared, 1)
                if m == SPREAD_AT + 1:
                    for c in range(CC):
                        if c % 2 == 0:
                            sc.wait_ge(ln_scaled, c // 2 + 1)
                        nc.scalar.activation(conv[:, c], conv[:, c], ACT.Silu, scale=par[:, G_LN + c:G_LN + c + 1],
                                             bias=par[:, B_LN + c:B_LN + c + 1]).then_inc(ln_silu, 1)
                if m == SPREAD_AT + 2:
                    for i in range(2):
                        sc.wait_ge(ln_silu, 4 * i + 4)
                        nc.scalar.activation(oT_hi[:, HEADS + 4 * i:HEADS + 4 * i + 4], conv[:, 4 * i:4 * i + 4],
                                             ACT.Copy).then_inc(convT_hi_ready, 1)
                for c in range(4):
                    if m == WO_B + 3 + 2 * c:
                        sc.wait_ge(panel_read, Q_WO_B + c + 1)
                        sum_squares(1, c)
                    if m == WO_B + 4 + 2 * c:
                        gain_hi(1, G_FFN, c, HIGH[0])

            def swish_of(done):
                sc.wait_ge(half_done, done)
                for t in range(TT):
                    ins = nc.scalar.activation(swish[:, t], LOW[0][t][:, :], ACT.Silu, scale=rstd[:, 1, t:t + 1])
                ins.then_inc(swish_ready, 1)

            def act_hi(j):
                sc.wait_ge(actT_turned, j + 1)
                for i in range(2):
                    ins = nc.scalar.activation(oT_hi[:, 2 * i:2 * i + 2], HIGH[0][i][:, :].rearrange("p (k t) -> p k t", k=2), ACT.Copy)
                ins.then_inc(actT_hi_ready, 1)

            def sigmoid_gate(c):
                for t in range(TT):
                    sc.wait_ge(gate_in, 2 * c + t + 1)
                    nc.scalar.activation(gate_p[:, t], gate_p[:, t], ACT.Sigmoid).then_inc(gate_p_ready, 1)

            for m in range(IN0, LOOP0):
                step(m)
                if m == FFN0 + 8:
                    sc.wait_ge(rstd_ready, 3)
                    swish_of(m)
                split_hi(m + AHEAD)
            with sc.Fori(0, LOOPS) as it:
                for t in range(PER_LOOP):
                    if t == 2:
                        act_hi(it)
                    if t == 8:
                        sc.wait_ge(act_ready, it + 1)
                        swish_of(LOOP0 + 8 + PER_LOOP * it)
                    split_hi(LOOP0 + t + AHEAD, it)
            for m in range(PLE0, END):
                if m == PLE0 + 2:
                    act_hi(LOOPS)
                if m in (PLE0 + 2, PLE0 + 4):
                    sc.wait_ge(half_done, m)
                    for c in range(m - PLE0 - 2, m - PLE0):
                        for t in range(TT):
                            ins = nc.scalar.activation(pw[:, t, c * NP:(c + 1) * NP], LOW[c % 2][t][:, :], ACT.Copy)
                        ins.then_inc(pw_ready, 1)
                for c in range(4):
                    if m == DOWN0 + 3 + 2 * c:
                        sc.wait_ge(panel_read, Q_DOWN_LAST + c + 1)
                        sum_squares(2, c)
                    if m == DOWN0 + 4 + 2 * c:
                        gain_hi(2, G_PLE, c, LOW[0])
                for c in range(3):
                    if m == PG0 + 8 * (c + 1):
                        sigmoid_gate(c)
                    if m == PG0 + 8 * (c + 1) + 3:
                        sc.wait_ge(h_ready, c + 1)
                        sum_squares(3, c)
                if m + AHEAD < END:
                    split_hi(m + AHEAD)
            sigmoid_gate(3)
            sc.wait_ge(h_ready, 4)
            sum_squares(3, 3)
            sc.wait_ge(rstd_ready, 5)
            sc.wait_ge(hg_ready, 8)
            nc.scalar.activation(h[:, 0], h[:, 0], ACT.Identity, scale=rstd[:, 3, 0:1]).then_inc(y_ready[0], 1)

        @block.vector
        def _(ve):
            def split_lo(m, it=0):
                ve.wait_ge(hi_ready, m + 1 + PER_LOOP * it)
                if m >= SLOTS:
                    ve.wait_ge(half_done, m - SLOTS + 1 + PER_LOOP * it)
                rows = slice(2 * (m % 2), 2 * (m % 2) + 2)
                nc.vector.tensor_tensor(w_lo[:, m % SLOTS], w_raw[:, (m // 2) % RAW, rows],
                                        w_hi[:, m % SLOTS].bitcast(F32), ALU.subtract).then_inc(lo_ready, 1)

            def gain_lo(norm, g_at, c, banks):
                ve.wait_ge(nT_hi_ready, 4 * norm + c + 1)
                for k in range(4):
                    ins = nc.vector.scalar_tensor_tensor(
                        nT_lo[:, 4 * c + k], banks[k // 2][:, (k % 2) * T:(k % 2 + 1) * T],
                        par[:, g_at + 4 * c + k:g_at + 4 * c + k + 1], nT_hi[:, 4 * c + k].bitcast(F32),
                        ALU.mult, ALU.subtract)
                ins.then_inc(nT_ready, 1)

            def mean_square(norm, order):
                ve.wait_ge(sq_ready, 8 * (norm + 1))
                nc.vector.reduce_sum(msq[:, norm], sq[:, norm], axis=AX.X).then_inc(sum_ready, 1)
                ve.wait_ge(sum_ready, norm + 1)
                nc.vector.tensor_scalar(msq[:, norm], msq[:, norm], 1.0 / D, EPS, ALU.mult, ALU.add).then_inc(msq_ready, 1)

            def along_tokens(n):
                return rb[:, :].unsqueeze(1).broadcast_to([P, n, T])

            def add_panel(q, c, done, it=0):
                ve.wait_ge(half_done, done + PER_LOOP * it)
                for t in range(TT):
                    cols = slice(c * NP, (c + 1) * NP)
                    ins = nc.vector.tensor_tensor(h[:, t, cols], pair_of(q)[t][:, :], h[:, t, cols], ALU.add)
                ins.then_inc(panel_read, 1)

            def conv_ops(m):
                for g, (first, end) in enumerate(CONV_STEPS):
                    if first <= m < end:
                        n = end - first
                        for i in range(CONV_OPS * (m - first) // n, CONV_OPS * (m - first + 1) // n):
                            tap, c = i // 4, 4 * g + i % 4
                            if i == 0:
                                ve.wait_ge(u_ready, g + 1)
                                ve.wait_ge(pad_ready, 1)
                            src = u[:, c, tap:tap + T]
                            if tap == 0:
                                ins = nc.vector.tensor_scalar(conv[:, c], src, taps[:, c, 0:1],
                                                              par[:, B_DW + c:B_DW + c + 1], ALU.mult, ALU.add)
                            else:
                                ve.wait_ge(conv_step, CONV_OPS * g + i - 3)
                                ins = nc.vector.scalar_tensor_tensor(conv[:, c], src, taps[:, c, tap:tap + 1],
                                                                     conv[:, c], ALU.mult, ALU.add)
                            ins.then_inc(conv_step, 1)

            def mask_steps(m):
                if m == 5:
                    ve.wait_ge(dist_ready, 2)
                    nc.vector.tensor_scalar(dist4, dist, 3, None, ALU.bitwise_and).then_inc(mask_step, 1)
                    nc.vector.tensor_scalar(dist16, dist, 15, None, ALU.bitwise_and).then_inc(mask_step, 1)
                    nc.vector.tensor_scalar(branches, dist, float(P), None, ALU.is_le).then_inc(mask_step, 1)
                if m == 6:
                    ve.wait_ge(mask_step, 3)
                    nc.vector.scalar_tensor_tensor(branches, dist4, 0.0, branches, ALU.is_equal, ALU.add).then_inc(mask_step, 1)
                    ve.wait_ge(mask_step, 4)
                    nc.vector.scalar_tensor_tensor(branches, dist16, 0.0, branches, ALU.is_equal, ALU.add).then_inc(mask_step, 1)
                if m == 7:
                    ve.wait_ge(mask_step, 5)
                    nc.vector.scalar_tensor_tensor(count[:, :], dist, 0.0, branches, ALU.is_ge, ALU.mult).then_inc(mask_step, 1)
                    ve.wait_ge(mask_step, 6)
                    nc.vector.tensor_scalar(mask[:, :], count[:, :], 0.0, NEG, ALU.is_equal, ALU.mult).then_inc(mask_step, 1)

            def row_max(hd):
                ve.wait_ge(scores_ready, hd + 1)
                if hd == 0:
                    ve.wait_ge(mask_step, 7)
                if hd >= 2:
                    ve.wait_ge(exp_ready, hd - 1)
                for lo, hi, t in ((0, P, 0), (P, 384, 1)):
                    ins = nc.vector.tensor_tensor_reduce(
                        out=masked[:, hd % 2, lo:hi], in0=ps[4 + hd % 2][:, lo:hi], in1=mask[:, lo:hi],
                        scale=1.0, scalar=3 * NEG, op0=ALU.add, op1=ALU.max, accum_out=top[:, hd, t:t + 1])
                ins.then_inc(masked_ready, 1)
                ve.wait_ge(masked_ready, hd + 1)
                nc.vector.tensor_scalar(ntop[:, hd], top[:, hd], -SCALE, None, ALU.mult).then_inc(ntop_ready, 1)

            def normalise(hd):
                ve.wait_ge(exp_ready, hd + 1)
                for lo, hi, t in ((0, P, 0), (P, 384, 1)):
                    ins = nc.vector.tensor_tensor_reduce(
                        out=prob[:, hd % 2, lo:hi], in0=prob[:, hd % 2, lo:hi], in1=count[:, lo:hi],
                        scale=1.0, scalar=0.0, op0=ALU.mult, op1=ALU.add, accum_out=den[:, hd, t:t + 1])
                ins.then_inc(den_ready, 1)
                ve.wait_ge(den_ready, hd + 1)
                nc.vector.reciprocal(rden[:, hd], den[:, hd]).then_inc(rden_ready, 1)
                ve.wait_ge(rden_ready, hd + 1)
                for lo, hi, t in ((0, P, 0), (P, 384, 1)):
                    ins = nc.vector.tensor_scalar(prob[:, hd % 2, lo:hi], prob[:, hd % 2, lo:hi],
                                                  rden[:, hd, t:t + 1], None, ALU.mult)
                ins.then_inc(prob_ready, 1)

            def take_panel(q):
                name = IN_PANELS[q]
                kind, g = name[:-1], int(name[-1])
                ve.wait_ge(half_done, 8 * (q + 1))
                if q == 0:
                    ve.wait_ge(rb_ready, 1)
                if name == "q1":
                    ve.wait_ge(scores_ready, 4)
                if name == "cg1":
                    ve.wait_ge(u_ready, 1)
                for b in range(2):
                    bank = pair_of(q)[b]
                    if kind == "v":
                        ins = nc.vector.tensor_scalar(v_sb[:, b, g * NP:(g + 1) * NP], bank[:, :], rstd[:, 0, b:b + 1], None, ALU.mult)
                    else:
                        dst = {"q": qT[:, 2 * b:2 * b + 2], "k": kT[:, 2 * b:2 * b + 2], "cg": gate_c[:, 2 * b:2 * b + 2],
                               "cv": u[:, 4 * g + 2 * b:4 * g + 2 * b + 2, PAD:PAD + T]}[kind]
                        ins = nc.vector.tensor_tensor(dst, bank[:, :].rearrange("p (c t) -> p c t", c=2), along_tokens(2), ALU.mult)
                ins.then_inc(panel_read, 1)

            ve.wait_ge(par_turned, 1)
            nc.vector.tensor_copy(par[:, :], ps[3][:, 0:N_PAR]).then_inc(par_ready, 1)
            ve.wait_ge(par_ready, 1)
            gain_lo(0, G_MIX, 0, HIGH[0])
            for m in range(0, AHEAD, 2):
                split_lo(m)

            def step(m):
                for c in range(1, 4):
                    if m == 2 * c - 1:
                        gain_lo(0, G_MIX, c, HIGH[c % 2])
                if m == 3:
                    ve.wait_ge(small_turned, 1)
                    nc.vector.tensor_copy(taps[:, :, 0:TAPS], ps[2][:, 0:CC * 32].rearrange("p (c k) -> p c k", k=32)[:, :, 0:TAPS]).then_inc(taps_ready, 1)
                if m == 4:
                    ve.wait_ge(pleT_hi_ready, 1)
                    nc.vector.tensor_tensor(pleT_lo[:, :, :], ps[3][:, :].rearrange("p (k t) -> p k t", k=2),
                                            pleT_hi[:, :, :].bitcast(F32), ALU.subtract).then_inc(pleT_ready, 1)
                if m == 7:
                    mean_square(0, 0)
                mask_steps(m)
                if m == 9:
                    ve.wait_ge(rb_spread, 1)
                    nc.vector.tensor_copy(rb[:, :], ps[6][:, 0:T]).then_inc(rb_ready, 1)
                if m == 10:
                    take_panel(0)
                if 8 < m <= WO_A and m % 8 == 0:
                    take_panel(m // 8 - 1)
                for g in range(2):
                    if m == 16 * (g + 1) + 1:
                        ve.wait_ge(gate_c_ready, g + 1)
                        ve.wait_ge(panel_read, 2 * g + 2)
                        nc.vector.tensor_tensor(u[:, 4 * g:4 * g + 4, PAD:PAD + T], u[:, 4 * g:4 * g + 4, PAD:PAD + T],
                                                gate_c[:, :, :], ALU.mult).then_inc(u_ready, 1)
                conv_ops(m)
                for hd in range(HEADS):
                    if m == SCORES_AT[hd]:
                        row_max(hd)
                    if m == SCORES_AT[hd] + 1:
                        normalise(hd)
                    if m == VALUES_AT[hd]:
                        ve.wait_ge(oT_hi_ready, hd + 1)
                        nc.vector.tensor_tensor(oT_lo[:, hd], ps[7][:, 0:T], oT_hi[:, hd].bitcast(F32), ALU.subtract).then_inc(oT_ready, 1)
                ln_steps(m)
                for q, start, halves in ((Q_WO_A, WO_A, 2), (Q_WO_C, WO_C, 4), (Q_WO_B, WO_B, 2)):
                    for c in range(4):
                        if m == start + halves * (c + 1):
                            if q > Q_WO_A:
                                ve.wait_ge(panel_read, q + c - 3)
                            add_panel(q + c, c, m)
                for c in range(4):
                    if m == WO_B + 4 + 2 * c:
                        gain_lo(1, G_FFN, c, HIGH[0])
                if m == WO_B + 11:
                    mean_square(1, 2)

            def ln_steps(m):
                def wide(bank):
                    return bank[:, T:2 * T].unsqueeze(1).broadcast_to([P, 2, T])
                if m == MEAN_AT:
                    ve.wait_ge(mean_ready, 1)
                    for i in range(4):
                        c = slice(2 * i, 2 * i + 2)
                        nc.vector.tensor_tensor(conv[:, c], conv[:, c], wide(ps[7]), ALU.subtract).then_inc(centered, 1)
                if m == VAR_AT:
                    ve.wait_ge(var_ready, 1)
                    nc.vector.tensor_scalar(msq[:, 4], ps[7][:, T:T + TT], EPS, None, ALU.add).then_inc(msq_ready, 1)
                if m == SPREAD_AT:
                    ve.wait_ge(ln_spread, 1)
                    ve.wait_ge(centered, 4)
                    for i in range(4):
                        c = slice(2 * i, 2 * i + 2)
                        nc.vector.tensor_tensor(conv[:, c], conv[:, c], wide(ps[7]), ALU.mult).then_inc(ln_scaled, 1)
                if m == SPREAD_AT + 2:
                    for i in range(2):
                        ve.wait_ge(convT_hi_ready, i + 1)
                        nc.vector.tensor_tensor(oT_lo[:, HEADS + 4 * i:HEADS + 4 * i + 4], conv[:, 4 * i:4 * i + 4],
                                                oT_hi[:, HEADS + 4 * i:HEADS + 4 * i + 4].bitcast(F32), ALU.subtract).then_inc(convT_ready, 1)

            def swiglu(j, done):
                ve.wait_ge(half_done, done)
                ve.wait_ge(swish_ready, j + 1)
                for t in range(TT):
                    ins = nc.vector.scalar_tensor_tensor(act[:, t], LOW[1][t][:, :], rstd[:, 1, t:t + 1], swish[:, t], ALU.mult, ALU.mult)
                ins.then_inc(act_ready, 1)

            def act_lo(j):
                ve.wait_ge(actT_hi_ready, j + 1)
                for i in range(2):
                    ins = nc.vector.tensor_tensor(oT_lo[:, 2 * i:2 * i + 2], HIGH[0][i][:, :].rearrange("p (k t) -> p k t", k=2),
                                                  oT_hi[:, 2 * i:2 * i + 2].bitcast(F32), ALU.subtract)
                ins.then_inc(actT_ready, 1)

            for m in range(IN0, LOOP0):
                step(m)
                if m + AHEAD >= POOL_UNTIL or m % 2 == 0:
                    split_lo(m + AHEAD)
            swiglu(0, LOOP0)
            with ve.Fori(0, LOOPS) as it:
                for t in range(PER_LOOP):
                    if t == 2:
                        act_lo(it)
                    if t == 16:
                        ve.wait_ge(actT_turned, it + 1)
                        swiglu(it + 1, LOOP0 + 16 + PER_LOOP * it)
                    if t in (18, 20, 22):
                        c = (t - 18) // 2
                        ve.wait_ge(panel_read, Q_DOWN + c - 3 + 4 * it)
                        add_panel(Q_DOWN + c, c, LOOP0 + t, it)
                    split_lo(LOOP0 + t + AHEAD, it)
                ve.wait_ge(panel_read, Q_DOWN + 4 * it)
                add_panel(Q_DOWN + 3, 3, LOOP0 + PER_LOOP, it)

            def gate_input(c):
                ve.wait_ge(half_done, PG0 + 8 * (c + 1))
                if c:
                    ve.wait_ge(h_ready, c)
                else:
                    ve.wait_ge(rows_loaded, 32)
                    ve.wait_ge(rstd_ready, 4)
                cols = slice(c * NP, (c + 1) * NP)
                for t in range(TT):
                    ins = nc.vector.scalar_tensor_tensor(gate_p[:, t], pair_of(Q_PG + c)[t][:, :], rstd[:, 2, t:t + 1],
                                                         b_rows[:, cols], ALU.mult, ALU.add)
                    ins.then_inc(gate_in, 1)

            def gated_input(c):
                cols = slice(c * NP, (c + 1) * NP)
                for t in range(TT):
                    ve.wait_ge(gate_p_ready, 2 * c + t + 1)
                    nc.vector.tensor_tensor(gate_p[:, t], gate_p[:, t], pw[:, t, cols], ALU.mult).then_inc(gated, 1)
                for t in range(TT):
                    ve.wait_ge(gated, 2 * c + t + 1)
                    ins = nc.vector.tensor_tensor(h[:, t, cols], h[:, t, cols], gate_p[:, t], ALU.add)
                ins.then_inc(h_ready, 1)

            for m in range(PLE0, END):
                if m == PLE0 + 2:
                    act_lo(LOOPS)
                for c in range(4):
                    if m == DOWN0 + 2 * (c + 1):
                        ve.wait_ge(panel_read, Q_DOWN_LAST + c - 3)
                        add_panel(Q_DOWN_LAST + c, c, m)
                    if m == DOWN0 + 4 + 2 * c:
                        gain_lo(2, G_PLE, c, LOW[0])
                if m == DOWN0 + 11:
                    mean_square(2, 3)
                for c in range(3):
                    if m == PG0 + 8 * (c + 1):
                        gate_input(c)
                    if m == PG0 + 8 * (c + 1) + 1:
                        gated_input(c)
                if m + AHEAD < END:
                    split_lo(m + AHEAD)
            gate_input(3)
            gated_input(3)
            mean_square(3, 4)
            cols = slice(3 * NP, 4 * NP)
            for t in range(TT):
                nc.vector.tensor_tensor(h[:, t, cols], h[:, t, cols], gf_rows[:, cols], ALU.mult).then_inc(hg_ready, 1)
            ve.wait_ge(rstd_ready, 5)
            ve.wait_ge(hg_ready, 8)
            nc.vector.tensor_scalar(h[:, 1], h[:, 1], rstd[:, 3, 1:2], None, ALU.mult).then_inc(y_ready[1], 1)

        @block.tensor
        def _(pe):
            def arrived(m, it=0):
                by_vector, by_pool = lo_count(m, it)
                if by_pool is None:
                    pe.wait_ge(lo_ready, by_vector)
                else:
                    pe.wait_ge(lo_ready_pool, by_pool)

            def tokens_by_columns(m, banks, x_hi, x_lo, first, last, it=0):
                arrived(m, it)
                s = m % SLOTS
                for k in range(2):
                    for t in range(TT):
                        rows = slice(t * P, (t + 1) * P)
                        start, stop = first and k == 0, last and k == 1
                        nc.tensor.matmul(banks[t][:, :], x_hi[:, k, rows], w_hi[:, s, k], start=start, stop=False)
                        nc.tensor.matmul(banks[t][:, :], x_hi[:, k, rows], w_lo[:, s, k], start=False, stop=False)
                        ins = nc.tensor.matmul(banks[t][:, :], x_lo[:, k, rows], w_hi[:, s, k], start=False, stop=stop)
                ins.then_inc(half_done, 1)

            def columns_by_tokens(m, banks, x_hi, x_lo, first, last):
                arrived(m)
                s = m % SLOTS
                for k in range(2):
                    for c in range(4):
                        dst = banks[c // 2][:, (c % 2) * T:(c % 2 + 1) * T]
                        cols = slice(c * P, (c + 1) * P)
                        start, stop = first and k == 0 and c % 2 == 0, last and k == 1
                        nc.tensor.matmul(dst, w_hi[:, s, k, cols], x_hi[:, k], start=start, stop=False, skip_group_check=True)
                        nc.tensor.matmul(dst, w_hi[:, s, k, cols], x_lo[:, k], start=False, stop=False, skip_group_check=True)
                        ins = nc.tensor.matmul(dst, w_lo[:, s, k, cols], x_hi[:, k], start=False, stop=stop, skip_group_check=True)
                ins.then_inc(half_done, 1)

            def turn(src, c, banks):
                for k in range(4):
                    for t in range(TT):
                        at = (k % 2) * T + t * P
                        ins = nc.tensor.transpose(banks[k // 2][:, at:at + P], src[:, t, c * NP + k * P:c * NP + (k + 1) * P], ident[:, :])
                return ins

            def turn_h(norm, c, banks):
                turn(h, c, banks).then_inc(hT_done, 1)

            def scores(hd):
                g, i = hd // 4, hd % 4
                pe.wait_ge(panel_read, (6, 9)[g])
                if hd >= 2:
                    pe.wait_ge(masked_ready, hd - 1)
                bank = ps[4 + hd % 2]
                nc.tensor.matmul(bank[:, 0:P], qT[:, i, 0:P], kT[:, i, 0:P], start=True, stop=True)
                nc.tensor.matmul(bank[:, P:384], qT[:, i, P:T], kT[:, i, 0:T], start=True, stop=True).then_inc(scores_ready, 1)

            def turn_probs(hd):
                pe.wait_ge(prob_ready, hd + 1)
                if hd:
                    pe.wait_ge(probT_ready, hd)
                for b in range(3):
                    ins = nc.tensor.transpose(ps[6][:, b * P:(b + 1) * P], prob[:, hd % 2, b * P:(b + 1) * P], ident[:, :])
                ins.then_inc(probT_turned, 1)

            def values(hd):
                g, b = hd // 4, hd % 4
                pe.wait_ge(panel_read, (7, 10)[g])
                pe.wait_ge(probT_ready, hd + 1)
                if hd:
                    pe.wait_ge(oT_ready, hd)
                if hd == 4:
                    pe.wait_ge(msq_ready, 2)
                if hd == 5:
                    pe.wait_ge(ln_scaled, 4)
                cols = slice(hd * DH, (hd + 1) * DH)
                nc.tensor.matmul(ps[7][:, 0:P], v_sb[:, 0, cols], probT[:, b, 0:P], start=True, stop=True)
                nc.tensor.matmul(ps[7][:, P:T], v_sb[:, 0, cols], probT[:, b, P:2 * P], start=True, stop=False)
                nc.tensor.matmul(ps[7][:, P:T], v_sb[:, 1, cols], probT[:, b, 2 * P:3 * P], start=False, stop=True).then_inc(o_done, 1)

            def spread(norm, bank, at):
                for t in range(TT):
                    ins = nc.tensor.matmul(bank[:, at + t * P:at + (t + 1) * P], rstd[:, norm, t:t + 1].broadcast_to([P, P]),
                                           ident[:, :], start=True, stop=True)
                return ins

            def before(m):
                if m in (0, 1, 3, 5):
                    c = (m + 1) // 2
                    pe.wait_ge(x_loaded[c], 16)
                    if c >= 2:
                        pe.wait_ge(nT_ready, c - 1)
                    turn_h(0, c, HIGH[c % 2])
                if m == 3:
                    pe.wait_ge(small_loaded, 32)
                    pe.wait_ge(par_ready, 1)
                    for c in range(CC):
                        nc.tensor.transpose(ps[2][:, c * 32:c * 32 + TAPS], taps_raw[0:TAPS, c * P:(c + 1) * P], ident[0:TAPS, 0:TAPS])
                    for k in range(2):
                        for t in range(TT):
                            at = k * T + t * P
                            ins = nc.tensor.transpose(ps[3][:, at:at + P], p_raw[:, t, k * P:(k + 1) * P], ident[:, :])
                    ins.then_inc(small_turned, 1)
                if m < 8 and m % 2 == 0:
                    pe.wait_ge(nT_ready, m // 2 + 1)
                if m == 9:
                    pe.wait_ge(rstd_ready, 1)
                    spread(0, ps[6], 0).then_inc(rb_spread, 1)
                if m == 10:
                    pe.wait_ge(rb_ready, 1)
                if m == 8:
                    pe.wait_ge(taps_ready, 1)
                    pe.wait_ge(pleT_ready, 1)
                for hd in range(HEADS):
                    if m == SCORES_AT[hd]:
                        scores(hd)
                    if m == TURN_AT[hd]:
                        turn_probs(hd)
                    if m == VALUES_AT[hd]:
                        values(hd)
                if m == MEAN_AT:
                    pe.wait_ge(consts_ready, 1)
                    pe.wait_ge(oT_ready, 4)
                    for c in range(CC):
                        if c % 4 == 0:
                            pe.wait_ge(conv_step, 2 * CONV_OPS if c else CONV_OPS)
                        ins = nc.tensor.matmul(ps[7][:, T:2 * T], mean_w[:, :], conv[:, c], start=c == 0, stop=c == CC - 1)
                    ins.then_inc(mean_ready, 1)
                if m == VAR_AT:
                    pe.wait_ge(dev_squared, 4)
                    for t in range(TT):
                        for c in range(CC):
                            ins = nc.tensor.matmul(ps[7][:, T + t:T + t + 1], u[:, c, t * P:(t + 1) * P], mean_w[:, 0:1],
                                                   start=c == 0, stop=c == CC - 1)
                    ins.then_inc(var_ready, 1)
                if m == SPREAD_AT:
                    pe.wait_ge(rstd_ready, 2)
                    pe.wait_ge(oT_ready, 5)
                    spread(4, ps[7], T).then_inc(ln_spread, 1)
                if m == WO_A:
                    pe.wait_ge(oT_ready, 4)
                if m == WO_C:
                    pe.wait_ge(convT_ready, 2)
                if m == WO_B:
                    pe.wait_ge(oT_ready, HEADS)
                for c in range(4):
                    if m == WO_B + 4 + 2 * c:
                        pe.wait_ge(panel_read, Q_WO_B + c + 1)
                        pe.wait_ge(nT_ready, 4 + c)
                        turn_h(1, c, HIGH[0])
                    if m == FFN0 + 2 * c:
                        pe.wait_ge(nT_ready, 4 + c + 1)

            def turn_last(c):
                pe.wait_ge(panel_read, Q_DOWN_LAST + c + 1)
                if c:
                    pe.wait_ge(nT_ready, 8 + c)
                else:
                    pe.wait_ge(pw_ready, 3)
                turn_h(2, c, LOW[0])

            def turn_act(j):
                pe.wait_ge(act_ready, j + 1)
                pe.wait_ge(panel_read, Q_DOWN - 1 + 4 * j)
                turn(act, 0, HIGH[0]).then_inc(actT_turned, 1)

            pe.wait_ge(ident_ready, 2)
            pe.wait_ge(par_loaded, 16 * 6)
            nc.tensor.transpose(ps[3][:, 0:N_PAR], par_raw[0:N_PAR, :], ident[0:N_PAR, 0:N_PAR]).then_inc(par_turned, 1)
            for m in range(IN0, WO_A):
                before(m)
                q, k = m // 8, m % 8
                if k == 0 and q >= 2:
                    pe.wait_ge(panel_read, q - 1)
                product = tokens_by_columns if IN_PANELS[q][0] == "v" else columns_by_tokens
                rows = slice(2 * k, 2 * k + 2)
                product(m, pair_of(q), nT_hi[:, rows], nT_lo[:, rows], k == 0, k == 7)
            for q0, start, halves, k0 in ((Q_WO_A, WO_A, 2, 0), (Q_WO_C, WO_C, 4, HEADS), (Q_WO_B, WO_B, 2, 4)):
                for c in range(4):
                    for k in range(halves):
                        m = start + halves * c + k
                        before(m)
                        if k == 0:
                            pe.wait_ge(panel_read, q0 + c - 1)
                        rows = slice(k0 + 2 * k, k0 + 2 * k + 2)
                        tokens_by_columns(m, pair_of(q0 + c), oT_hi[:, rows], oT_lo[:, rows], k == 0, k == halves - 1)
            for m in range(FFN0, LOOP0):
                before(m)
                k = m % 8
                if k == 0:
                    pe.wait_ge(panel_read, Q_DOWN - 1 if m == FFN0 else Q_DOWN)
                rows = slice(2 * k, 2 * k + 2)
                tokens_by_columns(m, LOW[(m - FFN0) // 8], nT_hi[:, rows], nT_lo[:, rows], k == 0, k == 7)
            with pe.Fori(0, LOOPS) as it:
                pe.wait_ge(swish_ready, it + 1)
                for k in range(8):
                    if k == 2:
                        turn_act(it)
                    rows = slice(2 * k, 2 * k + 2)
                    tokens_by_columns(LOOP0 + k, LOW[0], nT_hi[:, rows], nT_lo[:, rows], k == 0, k == 7, it)
                pe.wait_ge(act_ready, it + 1)
                for k in range(8):
                    rows = slice(2 * k, 2 * k + 2)
                    tokens_by_columns(LOOP0 + 8 + k, LOW[1], nT_hi[:, rows], nT_lo[:, rows], k == 0, k == 7, it)
                pe.wait_ge(actT_ready, it + 1)
                for c in range(4):
                    pe.wait_ge(panel_read, Q_DOWN + c - 1 + 4 * it)
                    for k in range(2):
                        rows = slice(2 * k, 2 * k + 2)
                        tokens_by_columns(LOOP0 + 16 + 2 * c + k, pair_of(Q_DOWN + c), oT_hi[:, rows], oT_lo[:, rows], k == 0, k == 1, it)
            for c in range(2):
                if c == 0:
                    pe.wait_ge(swish_ready, FP)
                    pe.wait_ge(act_ready, FP)
                else:
                    turn_act(LOOPS)
                    pe.wait_ge(pw_ready, 2)
                for k in range(2):
                    m = PLE0 + 2 * c + k
                    arrived(m)
                    for f in range(2):
                        for t in range(TT):
                            rows = slice(t * P, (t + 1) * P)
                            dst = LOW[f][t][:, :]
                            nc.tensor.matmul(dst, pleT_hi[:, k, rows], w_hi[:, m % SLOTS, f], start=k == 0, stop=False)
                            nc.tensor.matmul(dst, pleT_hi[:, k, rows], w_lo[:, m % SLOTS, f], start=False, stop=False)
                            ins = nc.tensor.matmul(dst, pleT_lo[:, k, rows], w_hi[:, m % SLOTS, f], start=False, stop=k == 1)
                    ins.then_inc(half_done, 1)
            pe.wait_ge(actT_ready, FP)
            for c in range(4):
                pe.wait_ge(panel_read, Q_DOWN_LAST + c - 1)
                for k in range(2):
                    if k == 0 and c >= 2:
                        turn_last(c - 2)
                    rows = slice(2 * k, 2 * k + 2)
                    tokens_by_columns(DOWN0 + 2 * c + k, pair_of(Q_DOWN_LAST + c), oT_hi[:, rows], oT_lo[:, rows], k == 0, k == 1)
            for c in range(4):
                if c < 2:
                    pe.wait_ge(panel_read, Q_PG + c - 1)
                else:
                    pe.wait_ge(gate_in, 2 * (c - 1))
                for k in range(8):
                    if c == 0 and k in (0, 2):
                        turn_last(2 + k // 2)
                    if c == 0 and k % 2 == 0:
                        pe.wait_ge(nT_ready, 8 + k // 2 + 1)
                    rows = slice(2 * k, 2 * k + 2)
                    tokens_by_columns(PG0 + 8 * c + k, pair_of(Q_PG + c), nT_hi[:, rows], nT_lo[:, rows], k == 0, k == 7)


_INS = ["x", "p", "g_mix", "w_in", "w_dw", "b_dw", "g_conv_ln", "b_conv_ln", "w_out", "g_ffn",
        "w_gate", "w_up", "w_down", "g_ple", "w_pgate", "b_pgate", "w_ple", "g_final"]


def kernel(**inputs):
    import numpy as np
    import concourse.bacc as bacc
    from concourse.bass_utils import run_bass_kernel_spmd

    nc = bacc.Bacc("TRN2", target_bir_lowering=False, num_devices=1)
    arrays, args = {}, []
    for name in _INS:
        a = np.ascontiguousarray(inputs[name])
        arrays[f"in_{name}"] = a
        args.append(nc.dram_tensor(f"in_{name}", a.shape, mybir.dt.from_np(a.dtype), kind="ExternalInput").ap())
    out = nc.dram_tensor("out", (1, T, D), F32, kind="ExternalOutput").ap()
    hybrid_decoder_layer(nc, *args, out)
    r = run_bass_kernel_spmd(nc, [arrays], core_ids=[0])
    return r.results[0]["out"]
```

```python
import concourse.bass as bass
from concourse import mybir
from contextlib import ExitStack

F32 = mybir.dt.float32
F32R = mybir.dt.float32r
I32 = mybir.dt.int32
ALU = mybir.AluOpType
ACT = mybir.ActivationFunctionType
AX = mybir.AxisListType

P = 128
T = 256
TT = T // P
D = 2048
KC = D // P
NP = 512
HEADS, DH = 8, 128
D_ATTN = HEADS * DH
D_CONV = D - D_ATTN
CC = D_CONV // P
TAPS = 31
PAD = TAPS - 1
D_FF = 5632
FP = D_FF // NP
D_PLE = 256
EPS = 1e-6
SCALE = float(DH) ** -0.5
NEG = -1e30

IN0 = 0
IN_PANELS = ["cv0", "cg0", "cv1", "cg1", "q0", "k0", "v0", "q1", "k1", "v1"]
IN_COLUMN = {"q": 0, "k": D_ATTN, "v": 2 * D_ATTN, "cv": 3 * D_ATTN, "cg": 3 * D_ATTN + D_CONV}
WO_A = IN0 + 8 * len(IN_PANELS)
WO_B = WO_A + 8
WO_C = WO_B + 8
FFN0 = WO_C + 16
LOOP0 = FFN0 + 16
LOOPS = FP - 1
PER_LOOP = 24
PLE0 = LOOP0 + PER_LOOP * LOOPS
DOWN0 = PLE0 + 4
PG0 = DOWN0 + 8
END = PG0 + 32
RAW = 4
SLOTS = 4
AHEAD = SLOTS
LAST = END - 8
POOL_HALF, POOL_UNTIL = 20, WO_C

Q_WO_A, Q_WO_B, Q_WO_C = 10, 14, 18
Q_DOWN = 22
Q_DOWN_LAST = Q_DOWN + 4 * LOOPS
Q_PG = Q_DOWN_LAST + 4

SCORES_AT = {h: (49 + 2 * h if h < 4 else 73 + 2 * (h - 4)) for h in range(HEADS)}
TURN_AT = {h: SCORES_AT[h] + 4 for h in range(HEADS)}
VALUES_AT = {0: 60, 1: 63, 2: 66, 3: 69, 4: 81, 5: 82, 6: 84, 7: 85}

CONV_STEPS = [(18, 48), (48, 84)]
CONV_OPS = 4 * (TAPS - 1)
MEAN_AT, VAR_AT, SPREAD_AT = 85, 88, 89

G_MIX, G_FFN, G_PLE, B_DW, G_LN, B_LN, N_PAR = 0, 16, 32, 48, 56, 64, 72


def by_pool(m):
    return m < POOL_UNTIL and (m % 4 == 3 or m % 2 == 1 and m >= POOL_HALF)


def lo_count(m, it=0):
    return sum(by_pool(i) == by_pool(m) for i in range(m + 1)) + PER_LOOP * it


def taps_done(g, m):
    first, end = CONV_STEPS[g]
    weights = [2 if any(a <= i <= a + 2 for a in SCORES_AT.values()) else 3 for i in range(first, end)]
    return CONV_OPS * sum(weights[:m - first]) // sum(weights)


def splits_at(m):
    ahead = {LAST - 4: (0, 1), LAST - 3: (2, 3), LAST - 2: (4, 5), LAST - 1: (6,), LAST: (7,)}
    if m >= LAST - AHEAD:
        return [LAST + i for i in ahead.get(m, ())]
    return [m + AHEAD]


def hybrid_decoder_layer(nc, x, p, g_mix, w_in, w_dw, b_dw, g_conv_ln, b_conv_ln, w_out, g_ffn,
                         w_gate, w_up, w_down, g_ple, w_pgate, b_pgate, w_ple, g_final, out):
    x_rows = x[0].rearrange("(t p) d -> p t d", p=P)
    out_rows = out[0].rearrange("(t p) d -> p t d", p=P)
    p_rows = p[0, 0].rearrange("(t p) d -> p t d", p=P)

    def by_rows(w):
        return w[0].rearrange("(k p) n -> p k n", p=P)

    w_in_v, w_out_v, w_gate_v, w_up_v = by_rows(w_in), by_rows(w_out), by_rows(w_gate), by_rows(w_up)
    w_down_v, w_pgate_v, w_ple_v = by_rows(w_down), by_rows(w_pgate), by_rows(w_ple)

    with ExitStack() as ctx:
        def sb(name, shape, dt=F32):
            return ctx.enter_context(nc.sbuf_tensor(name, shape, dt))

        def sem(name):
            return ctx.enter_context(nc.semaphore(name))

        w_raw = sb("w_raw", [P, RAW, 4, NP])
        w_hi = sb("w_hi", [P, SLOTS, 2, NP], F32R)
        w_lo = sb("w_lo", [P, SLOTS, 2, NP], F32R)
        nT_hi = sb("nT_hi", [P, KC, T], F32R)
        nT_lo = sb("nT_lo", [P, KC, T], F32R)
        oT_hi = sb("oT_hi", [P, KC, T], F32R)
        oT_lo = sb("oT_lo", [P, KC, T], F32R)
        pleT_hi = sb("pleT_hi", [P, 2, T], F32R)
        pleT_lo = sb("pleT_lo", [P, 2, T], F32R)
        h = sb("h", [P, TT, D])
        ident = sb("ident", [P, P])
        mean_w = sb("mean_w", [P, P])
        par = sb("par", [P, N_PAR])
        taps = sb("taps", [P, CC, 32])
        rb = sb("rb", [P, T])
        count = sb("count", [P, 384])
        mask = sb("mask", [P, 384])
        junk = sb("junk", [P, NP])
        sq = sb("sq", [P, 4, TT, 4])
        msq = sb("msq", [P, 5, TT])
        rstd = sb("rstd", [P, 5, TT])
        power = sb("power", [P, TT])
        warm = sb("warm", [P, TT])
        q_scale = sb("q_scale", [P, TT])
        top = sb("top", [P, HEADS, TT])
        ntop = sb("ntop", [P, HEADS, TT])
        den = sb("den", [P, HEADS, TT])
        rden = sb("rden", [P, HEADS, TT])
        arena = sb("arena", [P, 11504])

        def part(at, *shape):
            n = 1
            for s in shape:
                n *= s
            v = arena[:, at:at + n]
            return v.rearrange("p (a b) -> p a b", b=shape[-1]) if len(shape) == 2 else v

        qT, kT = part(0, 4, T), part(1024, 4, T)
        v_sb = part(2048, TT, D_ATTN)
        u = part(4096, CC, PAD + T)
        conv = part(6384, CC, T)
        masked = part(8432, 2, 384)
        prob = part(9200, 2, 384)
        probT = part(9968, 4, 384)
        gate_c = part(9968, 4, T)
        pair_sum = sb("pair_sum", [P, 2, T])
        dist = part(8432, 384).bitcast(I32)
        dist4 = part(8816, 384).bitcast(I32)
        dist16 = part(9200, 384).bitcast(I32)
        branches = part(9584, 384)
        p_raw = part(6384, TT, D_PLE)
        taps_raw = part(6896, D_CONV)
        par_raw = part(7920, P)
        swish = part(0, TT, NP)
        act = part(1024, TT, NP)
        gate_p = part(0, TT, NP)
        pw = part(2048, TT, D)
        b_rows = part(6144, D)
        gf_rows = part(8192, D)

        ps = [ctx.enter_context(nc.psum_tensor(f"ps{i}", [P, NP], F32)) for i in range(8)]
        LOW = [(ps[0], ps[1]), (ps[2], ps[3])]
        HIGH = [(ps[4], ps[5]), (ps[6], ps[7])]

        PLE_BANKS = [LOW[0], LOW[1], HIGH[1], LOW[0]]

        def values_bank(hd):
            return ps[5] if hd in (5, 7) else ps[7]

        def pair_of(q):
            return LOW[q % 2] if q < Q_DOWN else HIGH[q % 2]

        spare_hi = oT_hi[:, :, :].rearrange("p (s k a) t -> p s k (a t)", k=2, a=2)
        spare_lo = oT_lo[:, :, :].rearrange("p (s k a) t -> p s k (a t)", k=2, a=2)

        def slot_of(m):
            if LAST <= m < LAST + 4:
                return spare_hi[:, m - LAST], spare_lo[:, m - LAST]
            return w_hi[:, m % SLOTS], w_lo[:, m % SLOTS]

        def slot_free(engine, m, it=0):
            if LAST <= m < LAST + 4:
                engine.wait_ge(half_done, PG0)
            elif m >= LAST + 4:
                engine.wait_ge(half_done, m - 2 * SLOTS + 1)
            elif m >= SLOTS:
                engine.wait_ge(half_done, m - SLOTS + 1 + PER_LOOP * it)

        raw_ready = [sem(f"raw_ready{i}") for i in range(RAW)]
        x_loaded = [sem(f"x_loaded{i}") for i in range(4)]
        par_loaded, small_loaded, rows_loaded = sem("par_loaded"), sem("small_loaded"), sem("rows_loaded")
        out_stored = [sem(f"out_stored{i}") for i in range(2 * TT)]
        hi_ready, lo_ready, lo_ready_pool = sem("hi_ready"), sem("lo_ready"), sem("lo_ready_pool")
        half_done = sem("half_done")
        panel_read = sem("panel_read")
        consts_ready, ident_ready, pad_ready, dist_ready = sem("consts_ready"), sem("ident_ready"), sem("pad_ready"), sem("dist_ready")
        par_turned, par_ready = sem("par_turned"), sem("par_ready")
        small_turned, taps_ready, pleT_hi_ready, pleT_ready = sem("small_turned"), sem("taps_ready"), sem("pleT_hi_ready"), sem("pleT_ready")
        mask_step = sem("mask_step")
        hT_done, nT_hi_ready, nT_ready = sem("hT_done"), sem("nT_hi_ready"), sem("nT_ready")
        sq_ready, sum_ready, msq_ready, rstd_ready = sem("sq_ready"), sem("sum_ready"), sem("msq_ready"), sem("rstd_ready")
        rb_spread, rb_ready, q_scale_ready = sem("rb_spread"), sem("rb_ready"), sem("q_scale_ready")
        gate_c_ready, u_ready = sem("gate_c_ready"), sem("u_ready")
        conv_step, tap0_ready, conv_added = sem("conv_step"), sem("tap0_ready"), sem("conv_added")
        mean_ready, centered, dev_squared, dev_added, var_ready = sem("mean_ready"), sem("centered"), sem("dev_squared"), sem("dev_added"), sem("var_ready")
        ln_spread, ln_scaled, ln_silu, convT_hi_ready, convT_ready = sem("ln_spread"), sem("ln_scaled"), sem("ln_silu"), sem("convT_hi_ready"), sem("convT_ready")
        scores_ready, masked_ready, ntop_ready, exp_ready = sem("scores_ready"), sem("masked_ready"), sem("ntop_ready"), sem("exp_ready")
        den_ready, rden_ready, prob_ready = sem("den_ready"), sem("rden_ready"), sem("prob_ready")
        probT_turned, probT_ready, o_done, oT_hi_ready, oT_ready = sem("probT_turned"), sem("probT_ready"), sem("o_done"), sem("oT_hi_ready"), sem("oT_ready")
        h_ready = sem("h_ready")
        table_loaded = sem("table_loaded")
        swish_ready, act_ready, actT_turned, actT_hi_ready, actT_ready = sem("swish_ready"), sem("act_ready"), sem("actT_turned"), sem("actT_hi_ready"), sem("actT_ready")
        pw_ready, gate_in, gate_p_ready, gated = sem("pw_ready"), sem("gate_in"), sem("gate_p_ready"), sem("gated")
        hg_ready, y_left_ready, y_right_ready, last_done = sem("hg_ready"), sem("y_left_ready"), sem("y_right_ready"), sem("last_done")

        block = ctx.enter_context(nc.Block())

        @block.sync
        def _(sp):
            def load(n, src, it=0, dst=None):
                if n >= RAW:
                    last = 2 * (n - RAW) + 1
                    if by_pool(last):
                        sp.wait_ge(lo_ready, lo_count(last - 1))
                        sp.wait_ge(lo_ready_pool, lo_count(last))
                    else:
                        sp.wait_ge(lo_ready, lo_count(last, it))
                sp.dma_start(w_raw[:, n % RAW] if dst is None else dst, src).then_inc(raw_ready[n % RAW], 16)

            sp.dma_start(par_raw[0:KC, :], g_mix[0].rearrange("(r c) -> r c", c=P)).then_inc(par_loaded, 16)
            n = 0
            for panel in IN_PANELS:
                column = IN_COLUMN[panel[:-1]] + NP * int(panel[-1])
                for k in range(4):
                    if n < 4:
                        cols = slice(n * NP, (n + 1) * NP)
                        sp.dma_start(h[:, :, cols], x_rows[:, :, cols]).then_inc(x_loaded[n], 16)
                    load(n, w_in_v[:, 4 * k:4 * k + 4, column:column + NP])
                    n += 1
            for blocks in ((0,), (1,), (2, 3)):
                for c in range(4):
                    for k in blocks:
                        load(n, w_out_v[:, 4 * k:4 * k + 4, c * NP:(c + 1) * NP])
                        n += 1
            for w in (w_gate_v, w_up_v):
                for k in range(4):
                    load(n, w[:, 4 * k:4 * k + 4, 0:NP])
                    n += 1
            sp.wait_ge(convT_ready, 2)
            sp.wait_ge(oT_ready, HEADS)
            sp.dma_start(b_rows, b_pgate[0].partition_broadcast(P)).then_inc(rows_loaded, 16)
            sp.dma_start(gf_rows, g_final.partition_broadcast(P)).then_inc(rows_loaded, 16)
            with sp.Fori(0, LOOPS) as it:
                for i, w in enumerate((w_gate_v, w_up_v)):
                    for k in range(4):
                        load(n + 4 * i + k, w[:, 4 * k:4 * k + 4, bass.ds(it * NP + NP, NP)], it)
                for c in range(4):
                    load(n + 8 + c, w_down_v[:, bass.ds(it * 4, 4), c * NP:(c + 1) * NP], it)
            n = PLE0 // 2
            for c in range(2):
                load(n, w_ple_v[:, :, 2 * c * NP:2 * (c + 1) * NP],
                     dst=w_raw[:, n % RAW].rearrange("p (k f) n -> p k (f n)", f=2))
                n += 1
            for c in range(4):
                load(n, w_down_v[:, 4 * LOOPS:4 * LOOPS + 4, c * NP:(c + 1) * NP])
                n += 1
            for c in range(4):
                for k in range(4):
                    load(n, w_pgate_v[:, 4 * k:4 * k + 4, c * NP:(c + 1) * NP])
                    n += 1
            for t in range(TT):
                for i, (ready, cols) in enumerate(((y_left_ready, slice(0, D // 2)), (y_right_ready, slice(D // 2, D)))):
                    sp.wait_ge(ready, t + 1)
                    sp.dma_start(out_rows[:, t, cols], h[:, t, cols]).then_inc(out_stored[2 * t + i], 16)
            for stored in out_stored:
                sp.wait_ge(stored, 16)

        @block.gpsimd
        def _(pool):
            nc.gpsimd.memset(ident[:, :], 0.0).then_inc(ident_ready, 1)
            nc.gpsimd.memset(mean_w[:, :], 1.0 / D_CONV).then_inc(consts_ready, 1)
            nc.gpsimd.memset(power[:, :], -0.5).then_inc(consts_ready, 1)
            pool.wait_ge(ident_ready, 1)
            nc.gpsimd.affine_select(out=ident[:, :], in_=ident[:, :], compare_op=ALU.not_equal, fill=1.0,
                                    base=0, pattern=[[-1, P]], channel_multiplier=1).then_inc(ident_ready, 1)
            nc.gpsimd.iota(dist[:, 0:P], pattern=[[-1, P]], base=0, channel_multiplier=1).then_inc(dist_ready, 1)
            nc.gpsimd.iota(dist[:, P:384], pattern=[[-1, T]], base=P, channel_multiplier=1).then_inc(dist_ready, 1)
            nc.gpsimd.memset(u[:, :, 0:PAD], 0.0).then_inc(pad_ready, 1)

            def root(norm, order, tiles=slice(0, TT)):
                if order == 0:
                    pool.wait_ge(consts_ready, 2)
                pool.wait_ge(msq_ready, order + 1)
                nc.gpsimd.tensor_tensor(rstd[:, norm, tiles], msq[:, norm, tiles], power[:, tiles], ALU.pow).then_inc(rstd_ready, 1)

            def split_lo(m):
                pool.wait_ge(hi_ready, m + 1)
                slot_free(pool, m)
                rows = slice(2 * (m % 2), 2 * (m % 2) + 2)
                nc.gpsimd.tensor_tensor(w_lo[:, m % SLOTS], w_raw[:, (m // 2) % RAW, rows],
                                        w_hi[:, m % SLOTS].bitcast(F32), ALU.subtract).then_inc(lo_ready_pool, 1)

            for m in filter(by_pool, range(POOL_UNTIL)):
                if m == AHEAD + 7:
                    root(0, 0)
                if m == AHEAD + 51:
                    pool.wait_ge(conv_step, CONV_OPS)
                    nc.gpsimd.tensor_tensor(pair_sum[:, :, :], conv[:, 0:2], conv[:, 2:4], ALU.add).then_inc(conv_added, 1)
                if m == AHEAD + MEAN_AT + 2:
                    root(4, 1)
                if m == AHEAD + MEAN_AT:
                    for i in range(2):
                        pool.wait_ge(dev_squared, 2 * i + 2)
                        nc.gpsimd.tensor_tensor(u[:, 4 * i:4 * i + 2, 0:T], u[:, 4 * i:4 * i + 2, 0:T],
                                                u[:, 4 * i + 2:4 * i + 4, 0:T], ALU.add).then_inc(dev_added, 1)
                    pool.wait_ge(dev_added, 2)
                    nc.gpsimd.tensor_tensor(u[:, 0:2, 0:T], u[:, 0:2, 0:T], u[:, 4:6, 0:T], ALU.add).then_inc(dev_added, 1)
                split_lo(m)
            root(1, 2)
            root(2, 3)
            pool.wait_ge(rows_loaded, 32)
            for c in range(3):
                pool.wait_ge(sq_ready, 8 * 3 + 2 * (c + 1))
                for t in range(TT):
                    cols = slice(c * NP, (c + 1) * NP)
                    nc.gpsimd.tensor_tensor(h[:, t, cols], h[:, t, cols], gf_rows[:, cols], ALU.mult).then_inc(hg_ready, 1)
            for t in range(TT):
                root(3, 4 + t, slice(t, t + 1))

        @block.scalar
        def _(sc):
            def split_hi(m, it=0):
                sc.wait_ge(raw_ready[(m // 2) % RAW], 16 * (m // 2 // RAW + 1) + 48 * it)
                slot_free(sc, m, it)
                rows = slice(2 * (m % 2), 2 * (m % 2) + 2)
                nc.scalar.activation(slot_of(m)[0], w_raw[:, (m // 2) % RAW, rows], ACT.Copy).then_inc(hi_ready, 1)

            squares = [0]

            def sum_squares(norm, c, tiles=range(TT)):
                for t in tiles:
                    if squares[0]:
                        sc.wait_ge(sq_ready, squares[0])
                    nc.scalar.activation(junk[:, :], h[:, t, c * NP:(c + 1) * NP], ACT.Square,
                                         accum_out=sq[:, norm, t, c:c + 1]).then_inc(sq_ready, 1)
                    squares[0] += 1

            def gain_hi(norm, g_at, c, banks):
                sc.wait_ge(hT_done, 4 * norm + c + 1)
                for k in range(4):
                    ins = nc.scalar.activation(nT_hi[:, 4 * c + k], banks[k // 2][:, (k % 2) * T:(k % 2 + 1) * T],
                                               ACT.Identity, scale=par[:, g_at + 4 * c + k:g_at + 4 * c + k + 1])
                ins.then_inc(nT_hi_ready, 1)

            def exps(hd):
                sc.wait_ge(ntop_ready, hd + 1)
                if hd >= 2:
                    sc.wait_ge(probT_turned, hd - 1)
                for lo, hi, t in ((0, P, 0), (P, 384, 1)):
                    ins = nc.scalar.activation(prob[:, hd % 2, lo:hi], masked[:, hd % 2, lo:hi], ACT.Exp,
                                               scale=q_scale[:, t:t + 1], bias=ntop[:, hd, t:t + 1])
                ins.then_inc(exp_ready, 1)

            def divide(hd):
                sc.wait_ge(rden_ready, hd + 1)
                for lo, hi, t in ((0, P, 0), (P, 384, 1)):
                    ins = nc.scalar.activation(prob[:, hd % 2, lo:hi], prob[:, hd % 2, lo:hi], ACT.Copy,
                                               scale=rden[:, hd, t:t + 1])
                ins.then_inc(prob_ready, 1)

            sc.wait_ge(consts_ready, 2)
            nc.scalar.activation(warm[:, :], power[:, :], ACT.Copy).then_inc(table_loaded, 1)
            sc.wait_ge(par_ready, 1)
            gain_hi(0, G_MIX, 0, HIGH[0])
            for m in range(AHEAD):
                if m == 2:
                    gain_hi(0, G_MIX, 1, HIGH[1])
                split_hi(m)
                if m == 0:
                    for at, v, rows in ((G_FFN, g_ffn, KC), (G_PLE, g_ple, KC), (B_DW, b_dw, CC),
                                        (G_LN, g_conv_ln, CC), (B_LN, b_conv_ln, CC)):
                        sc.dma_start(par_raw[at:at + rows, :], v[0].rearrange("(r c) -> r c", c=P)).then_inc(small_loaded, 16)
                    sc.dma_start(taps_raw[0:TAPS, :], w_dw[0, :, 0, :]).then_inc(small_loaded, 16)
                    sc.dma_start(p_raw[:, :, :], p_rows).then_inc(small_loaded, 16)

            def take_panel(q):
                kind, g = IN_PANELS[q][0], int(IN_PANELS[q][-1])
                sc.wait_ge(half_done, 8 * (q + 1))
                if IN_PANELS[q] == "q1":
                    sc.wait_ge(scores_ready, 4)
                for b in range(2):
                    bank = pair_of(q)[b]
                    if kind == "v":
                        ins = nc.scalar.activation(v_sb[:, b, g * NP:(g + 1) * NP], bank[:, :], ACT.Copy, scale=rstd[:, 0, b:b + 1])
                    else:
                        ins = nc.scalar.activation(qT[:, 2 * b:2 * b + 2], bank[:, :].rearrange("p (c t) -> p c t", c=2), ACT.Copy)
                ins.then_inc(panel_read, 1)

            def step(m):
                for c in range(4):
                    if c >= 2 and m == 2 * c - 2:
                        gain_hi(0, G_MIX, c, HIGH[c % 2])
                    if m == 2 * c:
                        sum_squares(0, c)
                if m == 6:
                    sc.wait_ge(small_turned, 1)
                    nc.scalar.activation(pleT_hi[:, :, :], ps[3][:, :].rearrange("p (k t) -> p k t", k=2),
                                         ACT.Copy).then_inc(pleT_hi_ready, 1)
                if 8 < m <= WO_A and m % 8 == 0 and IN_PANELS[m // 8 - 1][0] in "qv":
                    take_panel(m // 8 - 1)
                for g in range(2):
                    if m == CONV_STEPS[g][0]:
                        sc.wait_ge(u_ready, g + 1)
                        sc.wait_ge(pad_ready, 1)
                        sc.wait_ge(taps_ready, 1)
                        for c in range(4 * g, 4 * g + 4):
                            ins = nc.scalar.activation(conv[:, c], u[:, c, 0:T], ACT.Identity, scale=taps[:, c, 0:1],
                                                       bias=par[:, B_DW + c:B_DW + c + 1])
                        ins.then_inc(tap0_ready, 1)
                    if m == 16 * (g + 1):
                        sc.wait_ge(panel_read, 2 * g + 2)
                        nc.scalar.activation(gate_c[:, :, :], gate_c[:, :, :], ACT.Sigmoid).then_inc(gate_c_ready, 1)
                for hd in range(HEADS):
                    if m == SCORES_AT[hd] + 1:
                        exps(hd)
                    if m == SCORES_AT[hd] + 3:
                        divide(hd)
                    if m == TURN_AT[hd] + 1:
                        sc.wait_ge(probT_turned, hd + 1)
                        if hd >= 4:
                            sc.wait_ge(o_done, hd - 3)
                        nc.scalar.activation(probT[:, hd % 4], ps[6][:, 0:384], ACT.Copy).then_inc(probT_ready, 1)
                    if m == VALUES_AT[hd] + 1:
                        sc.wait_ge(o_done, hd + 1)
                        nc.scalar.activation(oT_hi[:, hd], values_bank(hd)[:, 0:T], ACT.Copy).then_inc(oT_hi_ready, 1)
                if m == MEAN_AT:
                    for i in range(4):
                        sc.wait_ge(centered, i + 1)
                        nc.scalar.activation(u[:, 2 * i:2 * i + 2, 0:T], conv[:, 2 * i:2 * i + 2],
                                             ACT.Square).then_inc(dev_squared, 1)
                if m == SPREAD_AT - 1:
                    sc.wait_ge(table_loaded, 1)
                    nc.scalar.activation(warm[:, :], power[:, :], ACT.Silu).then_inc(table_loaded, 1)
                if m in (SPREAD_AT + 1, SPREAD_AT + 2):
                    first = 4 * (m - SPREAD_AT - 1)
                    for c in range(first, first + 4):
                        if c % 2 == 0:
                            sc.wait_ge(ln_scaled, c // 2 + 1)
                        nc.scalar.activation(conv[:, c], conv[:, c], ACT.Silu, scale=par[:, G_LN + c:G_LN + c + 1],
                                             bias=par[:, B_LN + c:B_LN + c + 1]).then_inc(ln_silu, 1)
                if m == SPREAD_AT + 3:
                    for i in range(2):
                        sc.wait_ge(ln_silu, 4 * i + 4)
                        nc.scalar.activation(oT_hi[:, HEADS + 4 * i:HEADS + 4 * i + 4], conv[:, 4 * i:4 * i + 4],
                                             ACT.Copy).then_inc(convT_hi_ready, 1)
                for c in range(4):
                    if m == WO_C + 4 * (c + 1) + 1:
                        sc.wait_ge(panel_read, Q_WO_C + c + 1)
                        sum_squares(1, c)
                    if m == WO_C + 4 * (c + 1) + 2:
                        gain_hi(1, G_FFN, c, HIGH[0])

            def swish_of(done):
                sc.wait_ge(half_done, done)
                for t in range(TT):
                    ins = nc.scalar.activation(swish[:, t], LOW[0][t][:, :], ACT.Silu, scale=rstd[:, 1, t:t + 1])
                ins.then_inc(swish_ready, 1)

            def act_hi(j):
                sc.wait_ge(actT_turned, j + 1)
                for i in range(2):
                    ins = nc.scalar.activation(oT_hi[:, 2 * i:2 * i + 2], HIGH[0][i][:, :].rearrange("p (k t) -> p k t", k=2), ACT.Copy)
                ins.then_inc(actT_hi_ready, 1)

            def sigmoid_gate(c, tiles=range(TT)):
                for t in tiles:
                    sc.wait_ge(gate_in, 2 * c + t + 1)
                    nc.scalar.activation(gate_p[:, t], gate_p[:, t], ACT.Sigmoid).then_inc(gate_p_ready, 1)

            for m in range(IN0, LOOP0):
                step(m)
                if m == FFN0 + 8:
                    sc.wait_ge(rstd_ready, 3)
                    swish_of(m)
                split_hi(m + AHEAD)
            with sc.Fori(0, LOOPS) as it:
                for t in range(PER_LOOP):
                    if t == 2:
                        act_hi(it)
                    if t == 8:
                        sc.wait_ge(act_ready, it + 1)
                        swish_of(LOOP0 + 8 + PER_LOOP * it)
                    split_hi(LOOP0 + t + AHEAD, it)
            for m in range(PLE0, END):
                if m == PLE0 + 1:
                    act_hi(LOOPS)
                if m in (PLE0 + 2, PLE0 + 4):
                    sc.wait_ge(half_done, m)
                    for c in range(m - PLE0 - 2, m - PLE0):
                        for t in range(TT):
                            ins = nc.scalar.activation(pw[:, t, c * NP:(c + 1) * NP], PLE_BANKS[c][t][:, :], ACT.Copy)
                        ins.then_inc(pw_ready, 1)
                for c in range(4):
                    if m == DOWN0 + 3 + 2 * c:
                        sc.wait_ge(panel_read, Q_DOWN_LAST + c + 1)
                        sum_squares(2, c)
                    if m == DOWN0 + 4 + 2 * c:
                        gain_hi(2, G_PLE, c, LOW[0])
                for c in range(3):
                    if m == PG0 + 8 * (c + 1):
                        sigmoid_gate(c)
                    if m == PG0 + 8 * (c + 1) + 3:
                        sc.wait_ge(h_ready, c + 1)
                        sum_squares(3, c)
                for i in splits_at(m):
                    split_hi(i)
            for t in range(TT):
                sigmoid_gate(3, [t])
                sc.wait_ge(h_ready, 3 + t + 1)
                sum_squares(3, 3, [t])
                sc.wait_ge(rstd_ready, 5 + t)
                sc.wait_ge(hg_ready, 6 + t + 1)
                cols = slice(D // 2, D)
                nc.scalar.activation(h[:, t, cols], h[:, t, cols], ACT.Identity, scale=rstd[:, 3, t:t + 1]).then_inc(y_right_ready, 1)

        @block.vector
        def _(ve):
            def split_lo(m, it=0):
                ve.wait_ge(hi_ready, m + 1 + PER_LOOP * it)
                slot_free(ve, m, it)
                rows = slice(2 * (m % 2), 2 * (m % 2) + 2)
                hi, lo = slot_of(m)
                nc.vector.tensor_tensor(lo, w_raw[:, (m // 2) % RAW, rows], hi.bitcast(F32), ALU.subtract).then_inc(lo_ready, 1)

            def gain_lo(norm, g_at, c, banks):
                ve.wait_ge(nT_hi_ready, 4 * norm + c + 1)
                for k in range(4):
                    ins = nc.vector.scalar_tensor_tensor(
                        nT_lo[:, 4 * c + k], banks[k // 2][:, (k % 2) * T:(k % 2 + 1) * T],
                        par[:, g_at + 4 * c + k:g_at + 4 * c + k + 1], nT_hi[:, 4 * c + k].bitcast(F32),
                        ALU.mult, ALU.subtract)
                ins.then_inc(nT_ready, 1)

            def mean_square(norm, order):
                ve.wait_ge(sq_ready, 8 * (norm + 1))
                nc.vector.reduce_sum(msq[:, norm], sq[:, norm], axis=AX.X).then_inc(sum_ready, 1)
                ve.wait_ge(sum_ready, norm + 1)
                nc.vector.tensor_scalar(msq[:, norm], msq[:, norm], 1.0 / D, EPS, ALU.mult, ALU.add).then_inc(msq_ready, 1)

            def along_tokens(n):
                return rb[:, :].unsqueeze(1).broadcast_to([P, n, T])

            def add_panel(q, c, done, it=0):
                ve.wait_ge(half_done, done + PER_LOOP * it)
                for t in range(TT):
                    cols = slice(c * NP, (c + 1) * NP)
                    ins = nc.vector.tensor_tensor(h[:, t, cols], pair_of(q)[t][:, :], h[:, t, cols], ALU.add)
                ins.then_inc(panel_read, 1)

            def conv_ops(m):
                for g, (first, end) in enumerate(CONV_STEPS):
                    if first <= m < end:
                        for i in range(taps_done(g, m), taps_done(g, m + 1)):
                            tap, c = i // 4 + 1, 4 * g + i % 4
                            if i == 0:
                                ve.wait_ge(tap0_ready, g + 1)
                            if i >= 4:
                                ve.wait_ge(conv_step, CONV_OPS * g + i - 3)
                            ins = nc.vector.scalar_tensor_tensor(conv[:, c], u[:, c, tap:tap + T], taps[:, c, tap:tap + 1],
                                                                 conv[:, c], ALU.mult, ALU.add)
                            ins.then_inc(conv_step, 1)

            def mask_steps(m):
                if m == 5:
                    ve.wait_ge(dist_ready, 2)
                    nc.vector.tensor_scalar(dist4, dist, 3, None, ALU.bitwise_and).then_inc(mask_step, 1)
                    nc.vector.tensor_scalar(dist16, dist, 15, None, ALU.bitwise_and).then_inc(mask_step, 1)
                    nc.vector.tensor_scalar(branches, dist, float(P), None, ALU.is_le).then_inc(mask_step, 1)
                if m == 6:
                    ve.wait_ge(mask_step, 3)
                    nc.vector.scalar_tensor_tensor(branches, dist4, 0.0, branches, ALU.is_equal, ALU.add).then_inc(mask_step, 1)
                    ve.wait_ge(mask_step, 4)
                    nc.vector.scalar_tensor_tensor(branches, dist16, 0.0, branches, ALU.is_equal, ALU.add).then_inc(mask_step, 1)
                if m == 7:
                    ve.wait_ge(mask_step, 5)
                    nc.vector.scalar_tensor_tensor(count[:, :], dist, 0.0, branches, ALU.is_ge, ALU.mult).then_inc(mask_step, 1)
                    ve.wait_ge(mask_step, 6)
                    nc.vector.tensor_scalar(mask[:, :], count[:, :], 0.0, NEG, ALU.is_equal, ALU.mult).then_inc(mask_step, 1)

            def row_max(hd):
                ve.wait_ge(scores_ready, hd + 1)
                if hd == 0:
                    ve.wait_ge(mask_step, 7)
                    ve.wait_ge(q_scale_ready, 1)
                if hd >= 2:
                    ve.wait_ge(exp_ready, hd - 1)
                for lo, hi, t in ((0, P, 0), (P, 384, 1)):
                    ins = nc.vector.tensor_tensor_reduce(
                        out=masked[:, hd % 2, lo:hi], in0=ps[4 + hd % 2][:, lo:hi], in1=mask[:, lo:hi],
                        scale=1.0, scalar=3 * NEG, op0=ALU.add, op1=ALU.max, accum_out=top[:, hd, t:t + 1])
                ins.then_inc(masked_ready, 1)
                ve.wait_ge(masked_ready, hd + 1)
                nc.vector.scalar_tensor_tensor(ntop[:, hd], top[:, hd], -1.0, q_scale[:, :], ALU.mult, ALU.mult).then_inc(ntop_ready, 1)

            def normalise(hd):
                ve.wait_ge(exp_ready, hd + 1)
                for lo, hi, t in ((0, P, 0), (P, 384, 1)):
                    ins = nc.vector.tensor_tensor_reduce(
                        out=prob[:, hd % 2, lo:hi], in0=prob[:, hd % 2, lo:hi], in1=count[:, lo:hi],
                        scale=1.0, scalar=0.0, op0=ALU.mult, op1=ALU.add, accum_out=den[:, hd, t:t + 1])
                ins.then_inc(den_ready, 1)
                ve.wait_ge(den_ready, hd + 1)
                nc.vector.reciprocal(rden[:, hd], den[:, hd]).then_inc(rden_ready, 1)

            def take_panel(q):
                name = IN_PANELS[q]
                kind, g = name[:-1], int(name[-1])
                ve.wait_ge(half_done, 8 * (q + 1))
                if q == 0:
                    ve.wait_ge(rb_ready, 1)
                if name == "k1":
                    ve.wait_ge(scores_ready, 4)
                if name == "cg1":
                    ve.wait_ge(u_ready, 1)
                for b in range(2):
                    dst = {"k": kT[:, 2 * b:2 * b + 2], "cg": gate_c[:, 2 * b:2 * b + 2],
                           "cv": u[:, 4 * g + 2 * b:4 * g + 2 * b + 2, PAD:PAD + T]}[kind]
                    ins = nc.vector.tensor_tensor(dst, pair_of(q)[b][:, :].rearrange("p (c t) -> p c t", c=2), along_tokens(2), ALU.mult)
                ins.then_inc(panel_read, 1)

            ve.wait_ge(par_turned, 1)
            nc.vector.tensor_copy(par[:, 0:KC], ps[3][:, 0:KC]).then_inc(par_ready, 1)
            ve.wait_ge(par_ready, 1)
            gain_lo(0, G_MIX, 0, HIGH[0])
            for m in range(AHEAD):
                if m == 2:
                    gain_lo(0, G_MIX, 1, HIGH[1])
                if not by_pool(m):
                    split_lo(m)

            def step(m):
                for c in range(2, 4):
                    if m == 2 * c - 2:
                        gain_lo(0, G_MIX, c, HIGH[c % 2])
                if m == 6:
                    ve.wait_ge(small_turned, 1)
                    nc.vector.tensor_copy(taps[:, :, 0:TAPS], ps[2][:, 0:CC * 32].rearrange("p (c k) -> p c k", k=32)[:, :, 0:TAPS])
                    nc.vector.tensor_copy(par[:, KC:N_PAR], ps[2][:, T + KC:T + N_PAR]).then_inc(taps_ready, 1)
                if m == 7:
                    ve.wait_ge(pleT_hi_ready, 1)
                    nc.vector.tensor_tensor(pleT_lo[:, :, :], ps[3][:, :].rearrange("p (k t) -> p k t", k=2),
                                            pleT_hi[:, :, :].bitcast(F32), ALU.subtract).then_inc(pleT_ready, 1)
                if m == 7:
                    mean_square(0, 0)
                mask_steps(m)
                if m == 9:
                    ve.wait_ge(rb_spread, 1)
                    nc.vector.tensor_scalar(q_scale[:, :], rstd[:, 0], SCALE, None, ALU.mult).then_inc(q_scale_ready, 1)
                    nc.vector.tensor_copy(rb[:, :], ps[6][:, 0:T]).then_inc(rb_ready, 1)
                if m == 10:
                    take_panel(0)
                if 8 < m <= WO_A and m % 8 == 0 and IN_PANELS[m // 8 - 1][0] in "ck":
                    take_panel(m // 8 - 1)
                for g in range(2):
                    if m == 16 * (g + 1) + 1:
                        ve.wait_ge(gate_c_ready, g + 1)
                        ve.wait_ge(panel_read, 2 * g + 2)
                        nc.vector.tensor_tensor(u[:, 4 * g:4 * g + 4, PAD:PAD + T], u[:, 4 * g:4 * g + 4, PAD:PAD + T],
                                                gate_c[:, :, :], ALU.mult).then_inc(u_ready, 1)
                for hd in range(HEADS):
                    if m == SCORES_AT[hd]:
                        row_max(hd)
                    if m == SCORES_AT[hd] + 2:
                        normalise(hd)
                    if m == VALUES_AT[hd] + (2 if hd < HEADS - 1 else 1):
                        ve.wait_ge(oT_hi_ready, hd + 1)
                        nc.vector.tensor_tensor(oT_lo[:, hd], values_bank(hd)[:, 0:T], oT_hi[:, hd].bitcast(F32), ALU.subtract).then_inc(oT_ready, 1)
                conv_ops(m)
                ln_steps(m)
                for q, start, halves in ((Q_WO_A, WO_A, 2), (Q_WO_B, WO_B, 2), (Q_WO_C, WO_C, 4)):
                    for c in range(4):
                        if m == start + halves * (c + 1):
                            if q > Q_WO_A:
                                ve.wait_ge(panel_read, q + c - 3)
                            add_panel(q + c, c, m)
                for c in range(4):
                    if m == WO_C + 4 * (c + 1) + 2:
                        gain_lo(1, G_FFN, c, HIGH[0])
                if m == FFN0 + 3:
                    mean_square(1, 2)

            def ln_steps(m):
                def wide(tokens):
                    return tokens.unsqueeze(1).broadcast_to([P, 2, T])
                if m == MEAN_AT:
                    ve.wait_ge(mean_ready, 1)
                    for i in range(4):
                        c = slice(2 * i, 2 * i + 2)
                        nc.vector.tensor_tensor(conv[:, c], conv[:, c], wide(ps[4][:, 0:T]), ALU.subtract).then_inc(centered, 1)
                if m == VAR_AT:
                    ve.wait_ge(var_ready, 1)
                    nc.vector.tensor_scalar(msq[:, 4], ps[4][:, 0:TT], EPS, None, ALU.add).then_inc(msq_ready, 1)
                if m == SPREAD_AT:
                    ve.wait_ge(ln_spread, 1)
                    ve.wait_ge(centered, 4)
                    for i in range(4):
                        c = slice(2 * i, 2 * i + 2)
                        nc.vector.tensor_tensor(conv[:, c], conv[:, c], wide(ps[4][:, 0:T]), ALU.mult).then_inc(ln_scaled, 1)
                if m == SPREAD_AT + 4:
                    for i in range(2):
                        ve.wait_ge(convT_hi_ready, i + 1)
                        nc.vector.tensor_tensor(oT_lo[:, HEADS + 4 * i:HEADS + 4 * i + 4], conv[:, 4 * i:4 * i + 4],
                                                oT_hi[:, HEADS + 4 * i:HEADS + 4 * i + 4].bitcast(F32), ALU.subtract).then_inc(convT_ready, 1)

            def swiglu(j, done):
                ve.wait_ge(half_done, done)
                ve.wait_ge(swish_ready, j + 1)
                for t in range(TT):
                    ins = nc.vector.scalar_tensor_tensor(act[:, t], LOW[1][t][:, :], rstd[:, 1, t:t + 1], swish[:, t], ALU.mult, ALU.mult)
                ins.then_inc(act_ready, 1)

            def act_lo(j):
                ve.wait_ge(actT_hi_ready, j + 1)
                for i in range(2):
                    ins = nc.vector.tensor_tensor(oT_lo[:, 2 * i:2 * i + 2], HIGH[0][i][:, :].rearrange("p (k t) -> p k t", k=2),
                                                  oT_hi[:, 2 * i:2 * i + 2].bitcast(F32), ALU.subtract)
                ins.then_inc(actT_ready, 1)

            for m in range(IN0, LOOP0):
                step(m)
                if not by_pool(m + AHEAD):
                    split_lo(m + AHEAD)
            swiglu(0, LOOP0)
            with ve.Fori(0, LOOPS) as it:
                for t in range(PER_LOOP):
                    if t == 2:
                        act_lo(it)
                    if t == 16:
                        ve.wait_ge(actT_turned, it + 1)
                        swiglu(it + 1, LOOP0 + 16 + PER_LOOP * it)
                    if t in (18, 20, 22):
                        c = (t - 18) // 2
                        ve.wait_ge(panel_read, Q_DOWN + c - 3 + 4 * it)
                        add_panel(Q_DOWN + c, c, LOOP0 + t, it)
                    split_lo(LOOP0 + t + AHEAD, it)
                ve.wait_ge(panel_read, Q_DOWN + 4 * it)
                add_panel(Q_DOWN + 3, 3, LOOP0 + PER_LOOP, it)

            def gate_input(c, tiles=range(TT)):
                if c:
                    ve.wait_ge(h_ready, c)
                else:
                    ve.wait_ge(rows_loaded, 32)
                    ve.wait_ge(rstd_ready, 4)
                for t in tiles:
                    nc.vector.scalar_tensor_tensor(gate_p[:, t], pair_of(Q_PG + c)[t][:, :], rstd[:, 2, t:t + 1],
                                                   b_rows[:, c * NP:(c + 1) * NP], ALU.mult, ALU.add).then_inc(gate_in, 1)

            def gated_input(c, tiles=range(TT)):
                cols = slice(c * NP, (c + 1) * NP)
                for t in tiles:
                    ve.wait_ge(gate_p_ready, 2 * c + t + 1)
                    nc.vector.tensor_tensor(gate_p[:, t], gate_p[:, t], pw[:, t, cols], ALU.mult).then_inc(gated, 1)
                for t in tiles:
                    ve.wait_ge(gated, 2 * c + t + 1)
                    ins = nc.vector.tensor_tensor(h[:, t, cols], h[:, t, cols], gate_p[:, t], ALU.add)
                ins.then_inc(h_ready, 1)

            for m in range(PLE0, END):
                if m == PLE0 + 1:
                    act_lo(LOOPS)
                for c in range(4):
                    if m == DOWN0 + 2 * (c + 1):
                        ve.wait_ge(panel_read, Q_DOWN_LAST + c - 3)
                        add_panel(Q_DOWN_LAST + c, c, m)
                    if m == DOWN0 + 4 + 2 * c:
                        gain_lo(2, G_PLE, c, LOW[0])
                if m == DOWN0 + 11:
                    mean_square(2, 3)
                for c in range(3):
                    if m == PG0 + 8 * (c + 1):
                        ve.wait_ge(half_done, m)
                        gate_input(c)
                    if m == PG0 + 8 * (c + 1) + 1:
                        gated_input(c)
                for i in splits_at(m):
                    split_lo(i)
            for t in range(TT):
                ve.wait_ge(last_done, t + 1)
                gate_input(3, [t])
                gated_input(3, [t])
                ve.wait_ge(sq_ready, 8 * 3 + 6 + t + 1)
                nc.vector.reduce_sum(msq[:, 3, t:t + 1], sq[:, 3, t], axis=AX.X).then_inc(sum_ready, 1)
                ve.wait_ge(sum_ready, 3 + t + 1)
                nc.vector.tensor_scalar(msq[:, 3, t:t + 1], msq[:, 3, t:t + 1], 1.0 / D, EPS, ALU.mult, ALU.add).then_inc(msq_ready, 1)
                cols = slice(3 * NP, 4 * NP)
                nc.vector.tensor_tensor(h[:, t, cols], h[:, t, cols], gf_rows[:, cols], ALU.mult).then_inc(hg_ready, 1)
                ve.wait_ge(rstd_ready, 5 + t)
                ve.wait_ge(hg_ready, 6 + t + 1)
                cols = slice(0, D // 2)
                nc.vector.tensor_scalar(h[:, t, cols], h[:, t, cols], rstd[:, 3, t:t + 1], None, ALU.mult).then_inc(y_left_ready, 1)

        @block.tensor
        def _(pe):
            def arrived(m, it=0):
                pe.wait_ge(lo_ready_pool if by_pool(m) else lo_ready, lo_count(m, it))

            def tokens_by_columns(m, banks, x_hi, x_lo, first, last, it=0):
                arrived(m, it)
                s = m % SLOTS
                for k in range(2):
                    for t in range(TT):
                        rows = slice(t * P, (t + 1) * P)
                        start, stop = first and k == 0, last and k == 1
                        nc.tensor.matmul(banks[t][:, :], x_hi[:, k, rows], w_hi[:, s, k], start=start, stop=False)
                        nc.tensor.matmul(banks[t][:, :], x_hi[:, k, rows], w_lo[:, s, k], start=False, stop=False)
                        ins = nc.tensor.matmul(banks[t][:, :], x_lo[:, k, rows], w_hi[:, s, k], start=False, stop=stop)
                ins.then_inc(half_done, 1)

            def columns_by_tokens(m, banks, x_hi, x_lo, first, last):
                arrived(m)
                s = m % SLOTS
                for k in range(2):
                    for c in range(4):
                        dst = banks[c // 2][:, (c % 2) * T:(c % 2 + 1) * T]
                        cols = slice(c * P, (c + 1) * P)
                        start, stop = first and k == 0 and c % 2 == 0, last and k == 1
                        nc.tensor.matmul(dst, w_hi[:, s, k, cols], x_hi[:, k], start=start, stop=False, skip_group_check=True)
                        nc.tensor.matmul(dst, w_hi[:, s, k, cols], x_lo[:, k], start=False, stop=False, skip_group_check=True)
                        ins = nc.tensor.matmul(dst, w_lo[:, s, k, cols], x_hi[:, k], start=False, stop=stop, skip_group_check=True)
                ins.then_inc(half_done, 1)

            def turn(src, c, banks):
                for k in range(4):
                    for t in range(TT):
                        at = (k % 2) * T + t * P
                        ins = nc.tensor.transpose(banks[k // 2][:, at:at + P], src[:, t, c * NP + k * P:c * NP + (k + 1) * P], ident[:, :])
                return ins

            def turn_h(norm, c, banks):
                turn(h, c, banks).then_inc(hT_done, 1)

            def scores(hd):
                g, i = hd // 4, hd % 4
                pe.wait_ge(panel_read, (6, 9)[g])
                if hd >= 2:
                    pe.wait_ge(masked_ready, hd - 1)
                bank = ps[4 + hd % 2]
                nc.tensor.matmul(bank[:, 0:P], qT[:, i, 0:P], kT[:, i, 0:P], start=True, stop=True)
                nc.tensor.matmul(bank[:, P:384], qT[:, i, P:T], kT[:, i, 0:T], start=True, stop=True).then_inc(scores_ready, 1)

            def turn_probs(hd):
                pe.wait_ge(prob_ready, hd + 1)
                if hd:
                    pe.wait_ge(probT_ready, hd)
                for b in range(3):
                    ins = nc.tensor.transpose(ps[6][:, b * P:(b + 1) * P], prob[:, hd % 2, b * P:(b + 1) * P], ident[:, :])
                ins.then_inc(probT_turned, 1)

            def values(hd):
                g, b = hd // 4, hd % 4
                pe.wait_ge(panel_read, (7, 10)[g])
                pe.wait_ge(probT_ready, hd + 1)
                if hd in (5, 7):
                    pe.wait_ge(masked_ready, HEADS)
                if hd:
                    pe.wait_ge(oT_ready, hd if hd <= 4 else hd - 1)
                bank = values_bank(hd)
                cols = slice(hd * DH, (hd + 1) * DH)
                nc.tensor.matmul(bank[:, 0:P], v_sb[:, 0, cols], probT[:, b, 0:P], start=True, stop=True)
                nc.tensor.matmul(bank[:, P:T], v_sb[:, 0, cols], probT[:, b, P:2 * P], start=True, stop=False)
                nc.tensor.matmul(bank[:, P:T], v_sb[:, 1, cols], probT[:, b, 2 * P:3 * P], start=False, stop=True).then_inc(o_done, 1)

            def spread(norm, bank, at):
                for t in range(TT):
                    ins = nc.tensor.matmul(bank[:, at + t * P:at + (t + 1) * P], rstd[:, norm, t:t + 1].broadcast_to([P, P]),
                                           ident[:, :], start=True, stop=True)
                return ins

            def before(m):
                for c in {0: (0, 1), 2: (2,), 4: (3,)}.get(m, ()):
                    pe.wait_ge(x_loaded[c], 16)
                    if c >= 2:
                        pe.wait_ge(nT_ready, c - 1)
                    turn_h(0, c, HIGH[c % 2])
                if m == 6:
                    pe.wait_ge(small_loaded, 16 * 7)
                    pe.wait_ge(par_ready, 1)
                    for c in range(CC):
                        nc.tensor.transpose(ps[2][:, c * 32:c * 32 + TAPS], taps_raw[0:TAPS, c * P:(c + 1) * P], ident[0:TAPS, 0:TAPS])
                    nc.tensor.transpose(ps[2][:, T:T + N_PAR], par_raw[0:N_PAR, :], ident[0:N_PAR, 0:N_PAR])
                    for k in range(2):
                        for t in range(TT):
                            at = k * T + t * P
                            ins = nc.tensor.transpose(ps[3][:, at:at + P], p_raw[:, t, k * P:(k + 1) * P], ident[:, :])
                    ins.then_inc(small_turned, 1)
                if m < 8 and m % 2 == 0:
                    pe.wait_ge(nT_ready, m // 2 + 1)
                if m == 9:
                    pe.wait_ge(rstd_ready, 1)
                    spread(0, ps[6], 0).then_inc(rb_spread, 1)
                if m == 10:
                    pe.wait_ge(rb_ready, 1)
                if m == 8:
                    pe.wait_ge(taps_ready, 1)
                    pe.wait_ge(pleT_ready, 1)
                for hd in range(HEADS):
                    if m == SCORES_AT[hd]:
                        scores(hd)
                    if m == TURN_AT[hd]:
                        turn_probs(hd)
                    if m == VALUES_AT[hd]:
                        values(hd)
                if m == MEAN_AT:
                    pe.wait_ge(consts_ready, 1)
                    pe.wait_ge(masked_ready, HEADS)
                    pe.wait_ge(conv_added, 1)
                    pe.wait_ge(conv_step, 2 * CONV_OPS)
                    chunks = [pair_sum[:, 0], pair_sum[:, 1]] + [conv[:, c] for c in range(4, CC)]
                    for i, chunk in enumerate(chunks):
                        ins = nc.tensor.matmul(ps[4][:, 0:T], mean_w[:, :], chunk, start=i == 0, stop=i == len(chunks) - 1)
                    ins.then_inc(mean_ready, 1)
                if m == VAR_AT:
                    pe.wait_ge(dev_added, 3)
                    for t in range(TT):
                        for c in range(2):
                            ins = nc.tensor.matmul(ps[4][:, t:t + 1], u[:, c, t * P:(t + 1) * P], mean_w[:, 0:1],
                                                   start=c == 0, stop=c == 1)
                    ins.then_inc(var_ready, 1)
                if m == SPREAD_AT:
                    pe.wait_ge(rstd_ready, 2)
                    spread(4, ps[4], 0).then_inc(ln_spread, 1)
                if m == WO_A:
                    pe.wait_ge(oT_ready, 4)
                if m in (WO_C, WO_C + 2):
                    pe.wait_ge(convT_ready, (m - WO_C) // 2 + 1)
                if m == WO_B:
                    pe.wait_ge(oT_ready, HEADS)
                for c in range(4):
                    if m == WO_C + 4 * (c + 1) + 2:
                        pe.wait_ge(panel_read, Q_WO_C + c + 1)
                        pe.wait_ge(nT_ready, 4 + c)
                        turn_h(1, c, HIGH[0])
                    if m == FFN0 + 2 * c:
                        pe.wait_ge(nT_ready, 4 + c + 1)

            def turn_last(c):
                pe.wait_ge(panel_read, Q_DOWN_LAST + c + 1)
                if c:
                    pe.wait_ge(nT_ready, 8 + c)
                else:
                    pe.wait_ge(pw_ready, 4)
                turn_h(2, c, LOW[0])

            def turn_act(j):
                pe.wait_ge(act_ready, j + 1)
                pe.wait_ge(panel_read, Q_DOWN - 1 + 4 * j)
                turn(act, 0, HIGH[0]).then_inc(actT_turned, 1)

            pe.wait_ge(ident_ready, 2)
            pe.wait_ge(par_loaded, 16)
            nc.tensor.transpose(ps[3][:, 0:KC], par_raw[0:KC, :], ident[0:KC, 0:KC]).then_inc(par_turned, 1)
            for m in range(IN0, WO_A):
                before(m)
                q, k = m // 8, m % 8
                if k == 0 and q >= 2:
                    pe.wait_ge(panel_read, q - 1)
                product = tokens_by_columns if IN_PANELS[q][0] == "v" else columns_by_tokens
                rows = slice(2 * k, 2 * k + 2)
                product(m, pair_of(q), nT_hi[:, rows], nT_lo[:, rows], k == 0, k == 7)
            for q0, start, halves, k0 in ((Q_WO_A, WO_A, 2, 0), (Q_WO_B, WO_B, 2, 4), (Q_WO_C, WO_C, 4, HEADS)):
                for c in range(4):
                    for k in range(halves):
                        m = start + halves * c + k
                        before(m)
                        if k == 0:
                            pe.wait_ge(panel_read, q0 + c - 1)
                        rows = slice(k0 + 2 * k, k0 + 2 * k + 2)
                        tokens_by_columns(m, pair_of(q0 + c), oT_hi[:, rows], oT_lo[:, rows], k == 0, k == halves - 1)
            for m in range(FFN0, LOOP0):
                before(m)
                k = m % 8
                if k == 0:
                    pe.wait_ge(panel_read, Q_DOWN - 1 if m == FFN0 else Q_DOWN)
                rows = slice(2 * k, 2 * k + 2)
                tokens_by_columns(m, LOW[(m - FFN0) // 8], nT_hi[:, rows], nT_lo[:, rows], k == 0, k == 7)
            with pe.Fori(0, LOOPS) as it:
                pe.wait_ge(swish_ready, it + 1)
                for k in range(8):
                    if k == 2:
                        turn_act(it)
                    rows = slice(2 * k, 2 * k + 2)
                    tokens_by_columns(LOOP0 + k, LOW[0], nT_hi[:, rows], nT_lo[:, rows], k == 0, k == 7, it)
                pe.wait_ge(act_ready, it + 1)
                for k in range(8):
                    rows = slice(2 * k, 2 * k + 2)
                    tokens_by_columns(LOOP0 + 8 + k, LOW[1], nT_hi[:, rows], nT_lo[:, rows], k == 0, k == 7, it)
                pe.wait_ge(actT_ready, it + 1)
                for c in range(4):
                    pe.wait_ge(panel_read, Q_DOWN + c - 1 + 4 * it)
                    for k in range(2):
                        rows = slice(2 * k, 2 * k + 2)
                        tokens_by_columns(LOOP0 + 16 + 2 * c + k, pair_of(Q_DOWN + c), oT_hi[:, rows], oT_lo[:, rows], k == 0, k == 1, it)
            for c in range(2):
                if c == 0:
                    pe.wait_ge(swish_ready, FP)
                    turn_act(LOOPS)
                else:
                    pe.wait_ge(panel_read, Q_DOWN_LAST)
                for k in range(2):
                    m = PLE0 + 2 * c + k
                    arrived(m)
                    for f in range(2):
                        if c == 1 and k == 0 and f == 1:
                            pe.wait_ge(pw_ready, 1)
                        for t in range(TT):
                            rows = slice(t * P, (t + 1) * P)
                            dst = PLE_BANKS[2 * c + f][t][:, :]
                            nc.tensor.matmul(dst, pleT_hi[:, k, rows], w_hi[:, m % SLOTS, f], start=k == 0, stop=False)
                            nc.tensor.matmul(dst, pleT_hi[:, k, rows], w_lo[:, m % SLOTS, f], start=False, stop=False)
                            ins = nc.tensor.matmul(dst, pleT_lo[:, k, rows], w_hi[:, m % SLOTS, f], start=False, stop=k == 1)
                    ins.then_inc(half_done, 1)
            pe.wait_ge(actT_ready, FP)
            for c in range(4):
                pe.wait_ge(panel_read, Q_DOWN_LAST + c - 1)
                if c == 1:
                    pe.wait_ge(pw_ready, 3)
                for k in range(2):
                    if k == 0 and c >= 2:
                        turn_last(c - 2)
                    rows = slice(2 * k, 2 * k + 2)
                    tokens_by_columns(DOWN0 + 2 * c + k, pair_of(Q_DOWN_LAST + c), oT_hi[:, rows], oT_lo[:, rows], k == 0, k == 1)
            for c in range(3):
                if c < 2:
                    pe.wait_ge(panel_read, Q_PG + c - 1)
                else:
                    pe.wait_ge(gate_in, 2 * (c - 1))
                for k in range(8):
                    if c == 0 and k in (0, 2):
                        turn_last(2 + k // 2)
                    if c == 0 and k % 2 == 0:
                        pe.wait_ge(nT_ready, 8 + k // 2 + 1)
                    rows = slice(2 * k, 2 * k + 2)
                    tokens_by_columns(PG0 + 8 * c + k, pair_of(Q_PG + c), nT_hi[:, rows], nT_lo[:, rows], k == 0, k == 7)
            pe.wait_ge(gate_in, 4)
            for t in range(TT):
                for m in range(LAST, END):
                    if t == 0:
                        arrived(m)
                    hi, lo = slot_of(m)
                    for k in range(2):
                        row = 2 * (m - LAST) + k
                        dst, tok = pair_of(Q_PG + 3)[t][:, :], slice(t * P, (t + 1) * P)
                        nc.tensor.matmul(dst, nT_hi[:, row, tok], hi[:, k], start=row == 0, stop=False)
                        nc.tensor.matmul(dst, nT_hi[:, row, tok], lo[:, k], start=False, stop=False)
                        ins = nc.tensor.matmul(dst, nT_lo[:, row, tok], hi[:, k], start=False, stop=row == KC - 1)
                ins.then_inc(last_done, 1)


_INS = ["x", "p", "g_mix", "w_in", "w_dw", "b_dw", "g_conv_ln", "b_conv_ln", "w_out", "g_ffn",
        "w_gate", "w_up", "w_down", "g_ple", "w_pgate", "b_pgate", "w_ple", "g_final"]


def kernel(**inputs):
    import numpy as np
    import concourse.bacc as bacc
    from concourse.bass_utils import run_bass_kernel_spmd

    nc = bacc.Bacc("TRN2", target_bir_lowering=False, num_devices=1)
    arrays, args = {}, []
    for name in _INS:
        a = np.ascontiguousarray(inputs[name])
        arrays[f"in_{name}"] = a
        args.append(nc.dram_tensor(f"in_{name}", a.shape, mybir.dt.from_np(a.dtype), kind="ExternalInput").ap())
    out = nc.dram_tensor("out", (1, T, D), F32, kind="ExternalOutput").ap()
    hybrid_decoder_layer(nc, *args, out)
    r = run_bass_kernel_spmd(nc, [arrays], core_ids=[0])
    return r.results[0]["out"]
```

```python
import concourse.bass as bass
from concourse import mybir
from contextlib import ExitStack

F32 = mybir.dt.float32
F32R = mybir.dt.float32r
I32 = mybir.dt.int32
ALU = mybir.AluOpType
ACT = mybir.ActivationFunctionType
AX = mybir.AxisListType

P = 128
T = 256
TT = T // P
D = 2048
KC = D // P
NP = 512
HEADS, DH = 8, 128
D_ATTN = HEADS * DH
D_CONV = D - D_ATTN
CC = D_CONV // P
TAPS = 31
PAD = TAPS - 1
D_FF = 5632
FP = D_FF // NP
D_PLE = 256
EPS = 1e-6
SCALE = float(DH) ** -0.5
NEG = -1e30

IN0 = 0
IN_PANELS = ["cv0", "cg0", "cv1", "cg1", "q0", "k0", "v0", "q1", "k1", "v1"]
IN_COLUMN = {"q": 0, "k": D_ATTN, "v": 2 * D_ATTN, "cv": 3 * D_ATTN, "cg": 3 * D_ATTN + D_CONV}
WO_A = IN0 + 8 * len(IN_PANELS)
WO_B = WO_A + 8
WO_C = WO_B + 8
FFN0 = WO_C + 16
LOOP0 = FFN0 + 16
LOOPS = FP - 1
PER_LOOP = 24
PLE0 = LOOP0 + PER_LOOP * LOOPS
DOWN0 = PLE0 + 4
PG0 = DOWN0 + 8
END = PG0 + 32
WARM_UPS = (6, 1, 3)
RAW = 4
SLOTS = 4
AHEAD = SLOTS
LAST = END - 8
LAST_PIECES = [(0, slice(0, NP)), (1, slice(0, NP // 2)), (1, slice(NP // 2, NP))]
OUT_PIECES = ([(0, right, slice(right * D // 2, (right + 1) * D // 2)) for right in (0, 1)]
              + [(1, right, slice(right * D // 2 + i * D // 4, right * D // 2 + (i + 1) * D // 4))
                 for i in range(2) for right in (0, 1)])
POOL_HALF, POOL_UNTIL = 40, WO_C

Q_WO_A, Q_WO_B, Q_WO_C = 10, 14, 18
Q_DOWN = 22
Q_DOWN_LAST = Q_DOWN + 4 * LOOPS
Q_PG = Q_DOWN_LAST + 4

SCORES_AT = {h: (49 + 2 * h if h < 4 else 73 + 2 * (h - 4)) for h in range(HEADS)}
TURN_AT = {h: SCORES_AT[h] + 4 for h in range(HEADS)}
VALUES_AT = {0: 60, 1: 64, 2: 68, 3: 72, 4: 81, 5: 82, 6: 84, 7: 85}

CONV_STEPS = [(18, 48), (48, 84)]
CONV_OPS = 4 * (TAPS - 1)
MEAN_AT, VAR_AT, SPREAD_AT = 85, 88, 89

G_MIX, G_FFN, G_PLE, B_DW, G_LN, B_LN, N_PAR = 0, 16, 32, 48, 56, 64, 72


def by_pool(m):
    return m < POOL_UNTIL and (m % 4 == 3 or m % 2 == 1 and m >= POOL_HALF)


def lo_count(m, it=0):
    return sum(by_pool(i) == by_pool(m) for i in range(m + 1)) + PER_LOOP * it


def taps_done(g, m):
    first, end = CONV_STEPS[g]
    weights = [1 if any(a - 2 <= i <= a + 2 for a in SCORES_AT.values()) else 2 for i in range(first, end)]
    return CONV_OPS * sum(weights[:m - first]) // sum(weights)


def splits_at(m):
    ahead = {LAST - 4: (0, 1), LAST - 3: (2, 3), LAST - 2: (4, 5), LAST - 1: (6,), LAST: (7,)}
    if m >= LAST - AHEAD:
        return [LAST + i for i in ahead.get(m, ())]
    return [m + AHEAD]


def hybrid_decoder_layer(nc, x, p, g_mix, w_in, w_dw, b_dw, g_conv_ln, b_conv_ln, w_out, g_ffn,
                         w_gate, w_up, w_down, g_ple, w_pgate, b_pgate, w_ple, g_final, out):
    x_rows = x[0].rearrange("(t p) d -> p t d", p=P)
    out_rows = out[0].rearrange("(t p) d -> p t d", p=P)
    p_rows = p[0, 0].rearrange("(t p) d -> p t d", p=P)

    def by_rows(w):
        return w[0].rearrange("(k p) n -> p k n", p=P)

    w_in_v, w_out_v, w_gate_v, w_up_v = by_rows(w_in), by_rows(w_out), by_rows(w_gate), by_rows(w_up)
    w_down_v, w_pgate_v, w_ple_v = by_rows(w_down), by_rows(w_pgate), by_rows(w_ple)

    with ExitStack() as ctx:
        def sb(name, shape, dt=F32):
            return ctx.enter_context(nc.sbuf_tensor(name, shape, dt))

        def sem(name):
            return ctx.enter_context(nc.semaphore(name))

        w_raw = sb("w_raw", [P, RAW, 4, NP])
        w_hi = sb("w_hi", [P, SLOTS, 2, NP], F32R)
        w_lo = sb("w_lo", [P, SLOTS, 2, NP], F32R)
        nT_hi = sb("nT_hi", [P, KC, T], F32R)
        nT_lo = sb("nT_lo", [P, KC, T], F32R)
        oT_hi = sb("oT_hi", [P, KC, T], F32R)
        oT_lo = sb("oT_lo", [P, KC, T], F32R)
        pleT_hi = sb("pleT_hi", [P, 2, T], F32R)
        pleT_lo = sb("pleT_lo", [P, 2, T], F32R)
        h = sb("h", [P, TT, D])
        ident = sb("ident", [P, P])
        mean_w = sb("mean_w", [P, P])
        par = sb("par", [P, N_PAR])
        taps = sb("taps", [P, CC, 32])
        rb = sb("rb", [P, T])
        count = sb("count", [P, 384])
        mask = sb("mask", [P, 384])
        junk = sb("junk", [P, NP])
        sq = sb("sq", [P, 4, TT, 5])
        msq = sb("msq", [P, 5, TT])
        rstd = sb("rstd", [P, 5, TT])
        power = sb("power", [P, TT])
        warm = sb("warm", [P, TT])
        q_scale = sb("q_scale", [P, TT])
        top = sb("top", [P, HEADS, TT])
        ntop = sb("ntop", [P, HEADS, TT])
        den = sb("den", [P, HEADS, TT])
        rden = sb("rden", [P, HEADS, TT])
        arena = sb("arena", [P, 11504])

        def part(at, *shape):
            n = 1
            for s in shape:
                n *= s
            v = arena[:, at:at + n]
            return v.rearrange("p (a b) -> p a b", b=shape[-1]) if len(shape) == 2 else v

        qT, kT = part(0, 4, T), part(1024, 4, T)
        v_sb = part(2048, TT, D_ATTN)
        u = part(4096, CC, PAD + T)
        conv = part(6384, CC, T)
        masked = part(8432, 2, 384)
        prob = part(9200, 2, 384)
        probT = part(9968, 4, 384)
        gate_c = part(9968, 4, T)
        group_sum = sb("group_sum", [P, 2, T])
        dist = part(8432, 384).bitcast(I32)
        dist4 = part(8816, 384).bitcast(I32)
        dist16 = part(9200, 384).bitcast(I32)
        branches = part(9584, 384)
        p_raw = part(6384, TT, D_PLE)
        taps_raw = part(6896, D_CONV)
        par_raw = part(7920, P)
        swish = part(0, TT, NP)
        act = part(1024, TT, NP)
        gate_p = part(0, TT, NP)
        pw = part(2048, TT, D)
        b_rows = part(6144, D)
        gf_rows = part(8192, D)

        ps = [ctx.enter_context(nc.psum_tensor(f"ps{i}", [P, NP], F32)) for i in range(8)]
        LOW = [(ps[0], ps[1]), (ps[2], ps[3])]
        HIGH = [(ps[4], ps[5]), (ps[6], ps[7])]

        PLE_BANKS = [LOW[0], LOW[1], HIGH[1], LOW[0]]

        SCORES_BANK, LN_BANK = ps[4], ps[5]

        def values_bank(hd):
            return SCORES_BANK if hd in (5, 7) else ps[7]

        def conv_sum(c):
            if c < 6:
                bank = ps[4] if c < 2 else ps[5]
                return bank[:, (c % 2) * T:(c % 2 + 1) * T]
            return conv[:, c]

        last_banks = [HIGH[1][0], HIGH[1][1], LOW[1][0]]

        def pair_of(q):
            return LOW[q % 2] if q < Q_DOWN else HIGH[q % 2]

        spare_hi = oT_hi[:, :, :].rearrange("p (s k a) t -> p s k (a t)", k=2, a=2)
        spare_lo = oT_lo[:, :, :].rearrange("p (s k a) t -> p s k (a t)", k=2, a=2)

        def slot_of(m):
            if LAST <= m < LAST + 4:
                return spare_hi[:, m - LAST], spare_lo[:, m - LAST]
            return w_hi[:, m % SLOTS], w_lo[:, m % SLOTS]

        def slot_free(engine, m, it=0):
            if LAST <= m < LAST + 4:
                engine.wait_ge(half_done, PG0)
            elif m >= LAST + 4:
                engine.wait_ge(half_done, m - 2 * SLOTS + 1)
            elif m >= SLOTS:
                engine.wait_ge(half_done, m - SLOTS + 1 + PER_LOOP * it)

        raw_ready = [sem(f"raw_ready{i}") for i in range(RAW)]
        raw_first, x_first, hT_first, nT_hi_first, nT_first = sem("raw_first"), sem("x_first"), sem("hT_first"), sem("nT_hi_first"), sem("nT_first")
        x_loaded = [sem(f"x_loaded{i}") for i in range(4)]
        par_loaded, small_loaded, rows_loaded = sem("par_loaded"), sem("small_loaded"), sem("rows_loaded")
        out_stored = [sem(f"out_stored{i}") for i in range(len(OUT_PIECES))]
        hi_ready, lo_ready, lo_ready_pool = sem("hi_ready"), sem("lo_ready"), sem("lo_ready_pool")
        half_done = sem("half_done")
        panel_read = sem("panel_read")
        consts_ready, ident_ready, pad_ready, dist_ready = sem("consts_ready"), sem("ident_ready"), sem("pad_ready"), sem("dist_ready")
        par_turned, par_ready = sem("par_turned"), sem("par_ready")
        small_turned, taps_ready, pleT_hi_ready, pleT_ready = sem("small_turned"), sem("taps_ready"), sem("pleT_hi_ready"), sem("pleT_ready")
        mask_step = sem("mask_step")
        hT_done, nT_hi_ready, nT_ready = sem("hT_done"), sem("nT_hi_ready"), sem("nT_ready")
        sq_ready, sum_ready, msq_ready, rstd_ready = sem("sq_ready"), sem("sum_ready"), sem("msq_ready"), sem("rstd_ready")
        rb_spread, rb_ready, q_scale_ready = sem("rb_spread"), sem("rb_ready"), sem("q_scale_ready")
        gate_c_ready, u_ready = sem("gate_c_ready"), sem("u_ready")
        conv_step, tap0_ready, conv_added = sem("conv_step"), sem("tap0_ready"), sem("conv_added")
        mean_ready, centered, dev_squared, dev_added, var_ready = sem("mean_ready"), sem("centered"), sem("dev_squared"), sem("dev_added"), sem("var_ready")
        ln_spread, ln_scaled, ln_silu, convT_hi_ready, convT_ready = sem("ln_spread"), sem("ln_scaled"), sem("ln_silu"), sem("convT_hi_ready"), sem("convT_ready")
        scores_ready, masked_ready, ntop_ready, exp_ready = sem("scores_ready"), sem("masked_ready"), sem("ntop_ready"), sem("exp_ready")
        den_ready, rden_ready, prob_ready = sem("den_ready"), sem("rden_ready"), sem("prob_ready")
        probT_turned, probT_ready, o_done, oT_hi_ready, oT_ready = sem("probT_turned"), sem("probT_ready"), sem("o_done"), sem("oT_hi_ready"), sem("oT_ready")
        h_ready = sem("h_ready")
        table_loaded = sem("table_loaded")
        swish_ready, act_ready, actT_turned, actT_hi_ready, actT_ready = sem("swish_ready"), sem("act_ready"), sem("actT_turned"), sem("actT_hi_ready"), sem("actT_ready")
        pw_ready, gate_in, gate_p_ready, gated = sem("pw_ready"), sem("gate_in"), sem("gate_p_ready"), sem("gated")
        hg_ready, hg_last_ready, y_left_ready, y_right_ready, last_done = sem("hg_ready"), sem("hg_last_ready"), sem("y_left_ready"), sem("y_right_ready"), sem("last_done")

        block = ctx.enter_context(nc.Block())

        @block.sync
        def _(sp):
            def load(n, src, it=0, dst=None):
                if n >= RAW:
                    last = 2 * (n - RAW) + 1
                    if by_pool(last):
                        sp.wait_ge(lo_ready, lo_count(last - 1))
                        sp.wait_ge(lo_ready_pool, lo_count(last))
                    else:
                        sp.wait_ge(lo_ready, lo_count(last, it))
                sp.dma_start(w_raw[:, n % RAW] if dst is None else dst, src).then_inc(raw_ready[n % RAW], 16)

            n = 0
            for panel in IN_PANELS:
                column = IN_COLUMN[panel[:-1]] + NP * int(panel[-1])
                for k in range(4):
                    if n == 0:
                        for rows, cols, x_sem, w_sem in ((slice(0, 2), slice(0, NP // 2), x_first, raw_first),
                                                         (slice(2, 4), slice(NP // 2, NP), x_loaded[0], raw_ready[0])):
                            sp.dma_start(h[:, :, cols], x_rows[:, :, cols]).then_inc(x_sem, 16)
                            sp.dma_start(w_raw[:, 0, rows], w_in_v[:, rows, column:column + NP]).then_inc(w_sem, 16)
                        n += 1
                        continue
                    if n < 4:
                        cols = slice(n * NP, (n + 1) * NP)
                        sp.dma_start(h[:, :, cols], x_rows[:, :, cols]).then_inc(x_loaded[n], 16)
                    if n == 4:
                        for at, v, rows in ((G_FFN, g_ffn, KC), (G_PLE, g_ple, KC), (B_DW, b_dw, CC),
                                            (G_LN, g_conv_ln, CC), (B_LN, b_conv_ln, CC)):
                            sp.dma_start(par_raw[at:at + rows, :], v[0].rearrange("(r c) -> r c", c=P)).then_inc(small_loaded, 16)
                        sp.dma_start(taps_raw[0:TAPS, :], w_dw[0, :, 0, :]).then_inc(small_loaded, 16)
                        sp.dma_start(p_raw[:, :, :], p_rows).then_inc(small_loaded, 16)
                    load(n, w_in_v[:, 4 * k:4 * k + 4, column:column + NP])
                    n += 1
            for blocks in ((0,), (1,), (2, 3)):
                for c in range(4):
                    for k in blocks:
                        load(n, w_out_v[:, 4 * k:4 * k + 4, c * NP:(c + 1) * NP])
                        n += 1
            for w in (w_gate_v, w_up_v):
                for k in range(4):
                    load(n, w[:, 4 * k:4 * k + 4, 0:NP])
                    n += 1
            sp.wait_ge(convT_ready, 2)
            sp.wait_ge(oT_ready, HEADS)
            sp.dma_start(b_rows, b_pgate[0].partition_broadcast(P)).then_inc(rows_loaded, 16)
            sp.dma_start(gf_rows, g_final.partition_broadcast(P)).then_inc(rows_loaded, 16)
            with sp.Fori(0, LOOPS) as it:
                for i, w in enumerate((w_gate_v, w_up_v)):
                    for k in range(4):
                        load(n + 4 * i + k, w[:, 4 * k:4 * k + 4, bass.ds(it * NP + NP, NP)], it)
                for c in range(4):
                    load(n + 8 + c, w_down_v[:, bass.ds(it * 4, 4), c * NP:(c + 1) * NP], it)
            n = PLE0 // 2
            for c in range(2):
                load(n, w_ple_v[:, :, 2 * c * NP:2 * (c + 1) * NP],
                     dst=w_raw[:, n % RAW].rearrange("p (k f) n -> p k (f n)", f=2))
                n += 1
            for c in range(4):
                load(n, w_down_v[:, 4 * LOOPS:4 * LOOPS + 4, c * NP:(c + 1) * NP])
                n += 1
            for c in range(4):
                for k in range(4):
                    load(n, w_pgate_v[:, 4 * k:4 * k + 4, c * NP:(c + 1) * NP])
                    n += 1
            for i, (t, right, cols) in enumerate(OUT_PIECES):
                sp.wait_ge(y_right_ready if right else y_left_ready, i // 2 + 1)
                sp.dma_start(out_rows[:, t, cols], h[:, t, cols]).then_inc(out_stored[i], 16)
            for stored in out_stored:
                sp.wait_ge(stored, 16)

        @block.gpsimd
        def _(pool):
            nc.gpsimd.memset(ident[:, :], 0.0).then_inc(ident_ready, 1)
            nc.gpsimd.memset(mean_w[:, :], 1.0 / D_CONV).then_inc(consts_ready, 1)
            nc.gpsimd.memset(power[:, :], -0.5).then_inc(consts_ready, 1)
            pool.wait_ge(ident_ready, 1)
            nc.gpsimd.affine_select(out=ident[:, :], in_=ident[:, :], compare_op=ALU.not_equal, fill=1.0,
                                    base=0, pattern=[[-1, P]], channel_multiplier=1).then_inc(ident_ready, 1)
            nc.gpsimd.iota(dist[:, 0:P], pattern=[[-1, P]], base=0, channel_multiplier=1).then_inc(dist_ready, 1)
            nc.gpsimd.iota(dist[:, P:384], pattern=[[-1, T]], base=P, channel_multiplier=1).then_inc(dist_ready, 1)
            nc.gpsimd.memset(u[:, :, 0:PAD], 0.0).then_inc(pad_ready, 1)

            def root(norm, order, tiles=slice(0, TT)):
                if order == 0:
                    pool.wait_ge(consts_ready, 2)
                pool.wait_ge(msq_ready, order + 1)
                nc.gpsimd.tensor_tensor(rstd[:, norm, tiles], msq[:, norm, tiles], power[:, tiles], ALU.pow).then_inc(rstd_ready, 1)

            def split_lo(m):
                pool.wait_ge(hi_ready, m + 1)
                slot_free(pool, m)
                rows = slice(2 * (m % 2), 2 * (m % 2) + 2)
                nc.gpsimd.tensor_tensor(w_lo[:, m % SLOTS], w_raw[:, (m // 2) % RAW, rows],
                                        w_hi[:, m % SLOTS].bitcast(F32), ALU.subtract).then_inc(lo_ready_pool, 1)

            for m in filter(by_pool, range(POOL_UNTIL)):
                if m == AHEAD + 7:
                    root(0, 0)
                if m == AHEAD + 51:
                    pool.wait_ge(conv_step, CONV_OPS)
                    nc.gpsimd.tensor_tensor(group_sum[:, :, :], conv[:, 0:2], conv[:, 2:4], ALU.add).then_inc(conv_added, 1)
                    pool.wait_ge(conv_added, 1)
                    nc.gpsimd.tensor_tensor(group_sum[:, 0], group_sum[:, 0], group_sum[:, 1], ALU.add).then_inc(conv_added, 1)
                if m == AHEAD + MEAN_AT - 2:
                    pool.wait_ge(conv_step, 2 * CONV_OPS)
                    nc.gpsimd.tensor_tensor(u[:, 4:6, 0:T], conv[:, 4:6], conv[:, 6:8], ALU.add).then_inc(conv_added, 1)
                    pool.wait_ge(conv_added, 3)
                    nc.gpsimd.tensor_tensor(group_sum[:, 1], u[:, 4, 0:T], u[:, 5, 0:T], ALU.add).then_inc(conv_added, 1)
                if m == AHEAD + MEAN_AT + 2:
                    root(4, 1)
                if m == AHEAD + MEAN_AT:
                    for i in range(2):
                        pool.wait_ge(dev_squared, 2 * i + 2)
                        nc.gpsimd.tensor_tensor(u[:, 4 * i:4 * i + 2, 0:T], u[:, 4 * i:4 * i + 2, 0:T],
                                                u[:, 4 * i + 2:4 * i + 4, 0:T], ALU.add).then_inc(dev_added, 1)
                    pool.wait_ge(dev_added, 2)
                    nc.gpsimd.tensor_tensor(u[:, 0:2, 0:T], u[:, 0:2, 0:T], u[:, 4:6, 0:T], ALU.add).then_inc(dev_added, 1)
                split_lo(m)
            root(1, 2)
            root(2, 3)
            pool.wait_ge(rows_loaded, 32)
            for c in range(3):
                pool.wait_ge(sq_ready, 8 * 3 + 2 * (c + 1))
                for t in range(TT):
                    cols = slice(c * NP, (c + 1) * NP)
                    nc.gpsimd.tensor_tensor(h[:, t, cols], h[:, t, cols], gf_rows[:, cols], ALU.mult).then_inc(hg_ready, 1)
            for t in range(TT):
                root(3, 4 + t, slice(t, t + 1))

        @block.scalar
        def _(sc):
            def split_hi(m, it=0):
                if m == 0:
                    sc.wait_ge(raw_first, 16)
                else:
                    sc.wait_ge(raw_ready[(m // 2) % RAW], 16 * (m // 2 // RAW + 1) + 48 * it)
                slot_free(sc, m, it)
                rows = slice(2 * (m % 2), 2 * (m % 2) + 2)
                nc.scalar.activation(slot_of(m)[0], w_raw[:, (m // 2) % RAW, rows], ACT.Copy).then_inc(hi_ready, 1)

            squares = [0]

            def sum_squares(norm, c):
                for t in range(TT):
                    square(norm, t, c, slice(c * NP, (c + 1) * NP))

            def square(norm, t, at, cols):
                if squares[0]:
                    sc.wait_ge(sq_ready, squares[0])
                nc.scalar.activation(junk[:, 0:cols.stop - cols.start], h[:, t, cols], ACT.Square,
                                     accum_out=sq[:, norm, t, at:at + 1]).then_inc(sq_ready, 1)
                squares[0] += 1

            def gain_hi(norm, g_at, c, banks, chunks=range(4)):
                first = chunks == range(2)
                sc.wait_ge(hT_first if first else hT_done, 4 * norm + c + 1)
                for k in chunks:
                    ins = nc.scalar.activation(nT_hi[:, 4 * c + k], banks[k // 2][:, (k % 2) * T:(k % 2 + 1) * T],
                                               ACT.Identity, scale=par[:, g_at + 4 * c + k:g_at + 4 * c + k + 1])
                ins.then_inc(nT_hi_first if first else nT_hi_ready, 1)

            def exps(hd):
                sc.wait_ge(ntop_ready, hd + 1)
                if hd >= 2:
                    sc.wait_ge(probT_turned, hd - 1)
                for lo, hi, t in ((0, P, 0), (P, 384, 1)):
                    ins = nc.scalar.activation(prob[:, hd % 2, lo:hi], masked[:, hd % 2, lo:hi], ACT.Exp,
                                               scale=q_scale[:, t:t + 1], bias=ntop[:, hd, t:t + 1])
                ins.then_inc(exp_ready, 1)

            def divide(hd):
                sc.wait_ge(rden_ready, hd + 1)
                for lo, hi, t in ((0, P, 0), (P, 384, 1)):
                    ins = nc.scalar.activation(prob[:, hd % 2, lo:hi], prob[:, hd % 2, lo:hi], ACT.Copy,
                                               scale=rden[:, hd, t:t + 1])
                ins.then_inc(prob_ready, 1)

            sc.dma_start(par_raw[0:KC, :], g_mix[0].rearrange("(r c) -> r c", c=P)).then_inc(par_loaded, 16)
            sc.wait_ge(consts_ready, 2)
            nc.scalar.activation(warm[:, :], power[:, :], ACT.Copy).then_inc(table_loaded, 1)
            sc.wait_ge(par_ready, 1)
            for m in range(AHEAD):
                if m < 2:
                    gain_hi(0, G_MIX, 0, HIGH[0], range(2 * m, 2 * m + 2))
                split_hi(m)
                if m == 2:
                    gain_hi(0, G_MIX, 1, HIGH[1])

            def take_panel(q):
                kind, g = IN_PANELS[q][0], int(IN_PANELS[q][-1])
                sc.wait_ge(half_done, 8 * (q + 1))
                if IN_PANELS[q] == "q1":
                    sc.wait_ge(scores_ready, 4)
                for b in range(2):
                    bank = pair_of(q)[b]
                    if kind == "v":
                        ins = nc.scalar.activation(v_sb[:, b, g * NP:(g + 1) * NP], bank[:, :], ACT.Copy, scale=rstd[:, 0, b:b + 1])
                    else:
                        ins = nc.scalar.activation(qT[:, 2 * b:2 * b + 2], bank[:, :].rearrange("p (c t) -> p c t", c=2), ACT.Copy)
                ins.then_inc(panel_read, 1)

            def step(m):
                for c in range(2, 4):
                    if m == 2 * c - 2:
                        gain_hi(0, G_MIX, c, HIGH[c % 2])
                if m in (1, 3, 5, 6):
                    sum_squares(0, m // 2)
                if m == 6:
                    sc.wait_ge(small_turned, 1)
                    nc.scalar.activation(pleT_hi[:, :, :], ps[3][:, :].rearrange("p (k t) -> p k t", k=2),
                                         ACT.Copy).then_inc(pleT_hi_ready, 1)
                if 8 < m <= WO_A and m % 8 == 0 and IN_PANELS[m // 8 - 1] in ("q0", "q1", "v1"):
                    take_panel(m // 8 - 1)
                for g in range(2):
                    if m == CONV_STEPS[g][0]:
                        sc.wait_ge(u_ready, g + 1)
                        sc.wait_ge(pad_ready, 1)
                        sc.wait_ge(taps_ready, 1)
                        if g:
                            sc.wait_ge(conv_step, CONV_OPS)
                        for c in range(4 * g, 4 * g + 4):
                            ins = nc.scalar.activation(conv_sum(c), u[:, c, 0:T], ACT.Identity, scale=taps[:, c, 0:1],
                                                       bias=par[:, B_DW + c:B_DW + c + 1])
                        ins.then_inc(tap0_ready, 1)
                    if m == 16 * (g + 1):
                        sc.wait_ge(panel_read, 2 * g + 2)
                        nc.scalar.activation(gate_c[:, :, :], gate_c[:, :, :], ACT.Sigmoid).then_inc(gate_c_ready, 1)
                for hd in range(HEADS):
                    if m == SCORES_AT[hd] + 1:
                        exps(hd)
                    if m == SCORES_AT[hd] + 3:
                        divide(hd)
                    if m == TURN_AT[hd] + 1:
                        sc.wait_ge(probT_turned, hd + 1)
                        if hd >= 4:
                            sc.wait_ge(o_done, hd - 3)
                        nc.scalar.activation(probT[:, hd % 4], ps[6][:, 0:384], ACT.Copy).then_inc(probT_ready, 1)
                    if m == VALUES_AT[hd] + 1:
                        sc.wait_ge(o_done, hd + 1)
                        nc.scalar.activation(oT_hi[:, hd], values_bank(hd)[:, 0:T], ACT.Copy).then_inc(oT_hi_ready, 1)
                if 8 < m <= WO_A and m % 8 == 0 and IN_PANELS[m // 8 - 1] == "v0":
                    take_panel(m // 8 - 1)
                if m == MEAN_AT:
                    for i in range(4):
                        sc.wait_ge(centered, i + 1)
                        nc.scalar.activation(u[:, 2 * i:2 * i + 2, 0:T], conv[:, 2 * i:2 * i + 2],
                                             ACT.Square).then_inc(dev_squared, 1)
                if m == SPREAD_AT - 1:
                    sc.wait_ge(table_loaded, 1)
                    nc.scalar.activation(warm[:, :], power[:, :], ACT.Silu).then_inc(table_loaded, 1)
                if m in (SPREAD_AT + 1, SPREAD_AT + 2):
                    first = 4 * (m - SPREAD_AT - 1)
                    for c in range(first, first + 4):
                        if c % 2 == 0:
                            sc.wait_ge(ln_scaled, c // 2 + 1)
                        nc.scalar.activation(conv[:, c], conv[:, c], ACT.Silu, scale=par[:, G_LN + c:G_LN + c + 1],
                                             bias=par[:, B_LN + c:B_LN + c + 1]).then_inc(ln_silu, 1)
                if m == SPREAD_AT + 3:
                    for i in range(2):
                        sc.wait_ge(ln_silu, 4 * i + 4)
                        nc.scalar.activation(oT_hi[:, HEADS + 4 * i:HEADS + 4 * i + 4], conv[:, 4 * i:4 * i + 4],
                                             ACT.Copy).then_inc(convT_hi_ready, 1)
                for c in range(4):
                    if m == WO_C + 4 * (c + 1) + 1:
                        sc.wait_ge(panel_read, Q_WO_C + c + 1)
                        sum_squares(1, c)
                    if m == WO_C + 4 * (c + 1) + 2:
                        gain_hi(1, G_FFN, c, HIGH[0])

            def swish_of(done):
                sc.wait_ge(half_done, done)
                for t in range(TT):
                    ins = nc.scalar.activation(swish[:, t], LOW[0][t][:, :], ACT.Silu, scale=rstd[:, 1, t:t + 1])
                ins.then_inc(swish_ready, 1)

            def act_hi(j):
                sc.wait_ge(actT_turned, j + 1)
                for i in range(2):
                    ins = nc.scalar.activation(oT_hi[:, 2 * i:2 * i + 2], HIGH[0][i][:, :].rearrange("p (k t) -> p k t", k=2), ACT.Copy)
                ins.then_inc(actT_hi_ready, 1)

            def sigmoid_gate(c):
                for t in range(TT):
                    sc.wait_ge(gate_in, 2 * c + t + 1)
                    nc.scalar.activation(gate_p[:, t], gate_p[:, t], ACT.Sigmoid).then_inc(gate_p_ready, 1)

            for m in range(IN0, LOOP0):
                step(m)
                if m == FFN0 + 8:
                    sc.wait_ge(rstd_ready, 3)
                    swish_of(m)
                split_hi(m + AHEAD)
            with sc.Fori(0, LOOPS) as it:
                for t in range(PER_LOOP):
                    if t == 2:
                        act_hi(it)
                    if t == 8:
                        sc.wait_ge(act_ready, it + 1)
                        swish_of(LOOP0 + 8 + PER_LOOP * it)
                    split_hi(LOOP0 + t + AHEAD, it)
            for m in range(PLE0, END):
                if m == PLE0 + 1:
                    act_hi(LOOPS)
                for c in {PLE0 + 1: (0,), PLE0 + 2: (1,), PLE0 + 4: (2, 3)}.get(m, ()):
                    sc.wait_ge(half_done, PLE0 + (2 if c < 2 else 4))
                    for t in range(TT):
                        ins = nc.scalar.activation(pw[:, t, c * NP:(c + 1) * NP], PLE_BANKS[c][t][:, :], ACT.Copy)
                    ins.then_inc(pw_ready, 1)
                for c in range(4):
                    if m == DOWN0 + 3 + 2 * c:
                        sc.wait_ge(panel_read, Q_DOWN_LAST + c + 1)
                        sum_squares(2, c)
                    if m == DOWN0 + 4 + 2 * c:
                        gain_hi(2, G_PLE, c, LOW[0])
                for c in range(3):
                    if m == PG0 + 8 * (c + 1):
                        sigmoid_gate(c)
                    if m == PG0 + 8 * (c + 1) + 3:
                        sc.wait_ge(h_ready, c + 1)
                        sum_squares(3, c)
                for i in splits_at(m):
                    split_hi(i)
            for i, (t, cols) in enumerate(LAST_PIECES):
                sc.wait_ge(gate_in, 6 + i + 1)
                nc.scalar.activation(gate_p[:, t, cols], gate_p[:, t, cols], ACT.Sigmoid).then_inc(gate_p_ready, 1)
                sc.wait_ge(h_ready, 3 + i + 1)
                square(3, t, 3 + cols.start * 2 // NP, slice(3 * NP + cols.start, 3 * NP + cols.stop))
                if cols.stop == NP:
                    sc.wait_ge(rstd_ready, 5 + t)
                    for tile, right, out_cols in OUT_PIECES:
                        if tile == t and right:
                            sc.wait_ge(hg_ready, 6)
                            sc.wait_ge(hg_last_ready, i + 1)
                            nc.scalar.activation(h[:, t, out_cols], h[:, t, out_cols], ACT.Identity,
                                                 scale=rstd[:, 3, t:t + 1]).then_inc(y_right_ready, 1)

        @block.vector
        def _(ve):
            def split_lo(m, it=0):
                ve.wait_ge(hi_ready, m + 1 + PER_LOOP * it)
                slot_free(ve, m, it)
                rows = slice(2 * (m % 2), 2 * (m % 2) + 2)
                hi, lo = slot_of(m)
                nc.vector.tensor_tensor(lo, w_raw[:, (m // 2) % RAW, rows], hi.bitcast(F32), ALU.subtract).then_inc(lo_ready, 1)

            def gain_lo(norm, g_at, c, banks, chunks=range(4)):
                first = chunks == range(2)
                ve.wait_ge(nT_hi_first if first else nT_hi_ready, 4 * norm + c + 1)
                for k in chunks:
                    ins = nc.vector.scalar_tensor_tensor(
                        nT_lo[:, 4 * c + k], banks[k // 2][:, (k % 2) * T:(k % 2 + 1) * T],
                        par[:, g_at + 4 * c + k:g_at + 4 * c + k + 1], nT_hi[:, 4 * c + k].bitcast(F32),
                        ALU.mult, ALU.subtract)
                ins.then_inc(nT_first if first else nT_ready, 1)

            def mean_square(norm, order):
                ve.wait_ge(sq_ready, 8 * (norm + 1))
                nc.vector.reduce_sum(msq[:, norm], sq[:, norm, :, 0:4], axis=AX.X).then_inc(sum_ready, 1)
                ve.wait_ge(sum_ready, norm + 1)
                nc.vector.tensor_scalar(msq[:, norm], msq[:, norm], 1.0 / D, EPS, ALU.mult, ALU.add).then_inc(msq_ready, 1)

            def along_tokens(n):
                return rb[:, :].unsqueeze(1).broadcast_to([P, n, T])

            def add_panel(q, c, done, it=0):
                ve.wait_ge(half_done, done + PER_LOOP * it)
                for t in range(TT):
                    cols = slice(c * NP, (c + 1) * NP)
                    ins = nc.vector.tensor_tensor(h[:, t, cols], pair_of(q)[t][:, :], h[:, t, cols], ALU.add)
                ins.then_inc(panel_read, 1)

            def conv_ops(m):
                for g, (first, end) in enumerate(CONV_STEPS):
                    if first <= m < end:
                        for i in range(taps_done(g, m), taps_done(g, m + 1)):
                            tap, c = i // 4 + 1, 4 * g + i % 4
                            if i == 0:
                                ve.wait_ge(tap0_ready, g + 1)
                            if i >= 4:
                                ve.wait_ge(conv_step, CONV_OPS * g + i - 3)
                            dst = conv[:, c] if tap == TAPS - 1 else conv_sum(c)
                            ins = nc.vector.scalar_tensor_tensor(dst, u[:, c, tap:tap + T], taps[:, c, tap:tap + 1],
                                                                 conv_sum(c), ALU.mult, ALU.add)
                            ins.then_inc(conv_step, 1)

            def mask_steps(m):
                if m == 5:
                    ve.wait_ge(dist_ready, 2)
                    nc.vector.tensor_scalar(dist4, dist, 3, None, ALU.bitwise_and).then_inc(mask_step, 1)
                    nc.vector.tensor_scalar(dist16, dist, 15, None, ALU.bitwise_and).then_inc(mask_step, 1)
                    nc.vector.tensor_scalar(branches, dist, float(P), None, ALU.is_le).then_inc(mask_step, 1)
                if m == 6:
                    ve.wait_ge(mask_step, 3)
                    nc.vector.scalar_tensor_tensor(branches, dist4, 0.0, branches, ALU.is_equal, ALU.add).then_inc(mask_step, 1)
                    ve.wait_ge(mask_step, 4)
                    nc.vector.scalar_tensor_tensor(branches, dist16, 0.0, branches, ALU.is_equal, ALU.add).then_inc(mask_step, 1)
                if m == 7:
                    ve.wait_ge(mask_step, 5)
                    nc.vector.scalar_tensor_tensor(count[:, :], dist, 0.0, branches, ALU.is_ge, ALU.mult).then_inc(mask_step, 1)
                    ve.wait_ge(mask_step, 6)
                    nc.vector.tensor_scalar(mask[:, :], count[:, :], 0.0, NEG, ALU.is_equal, ALU.mult).then_inc(mask_step, 1)

            def row_max(hd):
                ve.wait_ge(scores_ready, hd + 1)
                if hd == 0:
                    ve.wait_ge(mask_step, 7)
                    ve.wait_ge(q_scale_ready, 1)
                if hd >= 2:
                    ve.wait_ge(exp_ready, hd - 1)
                for lo, hi, t in ((0, P, 0), (P, 384, 1)):
                    ins = nc.vector.tensor_tensor_reduce(
                        out=masked[:, hd % 2, lo:hi], in0=SCORES_BANK[:, lo:hi], in1=mask[:, lo:hi],
                        scale=1.0, scalar=3 * NEG, op0=ALU.add, op1=ALU.max, accum_out=top[:, hd, t:t + 1])
                ins.then_inc(masked_ready, 1)
                ve.wait_ge(masked_ready, hd + 1)
                nc.vector.scalar_tensor_tensor(ntop[:, hd], top[:, hd], -1.0, q_scale[:, :], ALU.mult, ALU.mult).then_inc(ntop_ready, 1)

            def normalise(hd):
                ve.wait_ge(exp_ready, hd + 1)
                for lo, hi, t in ((0, P, 0), (P, 384, 1)):
                    ins = nc.vector.tensor_tensor_reduce(
                        out=prob[:, hd % 2, lo:hi], in0=prob[:, hd % 2, lo:hi], in1=count[:, lo:hi],
                        scale=1.0, scalar=0.0, op0=ALU.mult, op1=ALU.add, accum_out=den[:, hd, t:t + 1])
                ins.then_inc(den_ready, 1)
                ve.wait_ge(den_ready, hd + 1)
                nc.vector.reciprocal(rden[:, hd], den[:, hd]).then_inc(rden_ready, 1)

            def take_panel(q):
                name = IN_PANELS[q]
                kind, g = name[:-1], int(name[-1])
                ve.wait_ge(half_done, 8 * (q + 1))
                if q == 0:
                    ve.wait_ge(rb_ready, 1)
                if name == "k1":
                    ve.wait_ge(scores_ready, 4)
                if name == "cg1":
                    ve.wait_ge(u_ready, 1)
                for b in range(2):
                    dst = {"k": kT[:, 2 * b:2 * b + 2], "cg": gate_c[:, 2 * b:2 * b + 2],
                           "cv": u[:, 4 * g + 2 * b:4 * g + 2 * b + 2, PAD:PAD + T]}[kind]
                    ins = nc.vector.tensor_tensor(dst, pair_of(q)[b][:, :].rearrange("p (c t) -> p c t", c=2), along_tokens(2), ALU.mult)
                ins.then_inc(panel_read, 1)

            ve.wait_ge(par_turned, 1)
            nc.vector.tensor_copy(par[:, 0:KC], ps[3][:, 0:KC]).then_inc(par_ready, 1)
            ve.wait_ge(par_ready, 1)
            for m in range(AHEAD):
                if m < 2:
                    gain_lo(0, G_MIX, 0, HIGH[0], range(2 * m, 2 * m + 2))
                if not by_pool(m):
                    split_lo(m)
                if m == 2:
                    gain_lo(0, G_MIX, 1, HIGH[1])

            def step(m):
                for c in range(2, 4):
                    if m == 2 * c - 2:
                        gain_lo(0, G_MIX, c, HIGH[c % 2])
                if m == 6:
                    ve.wait_ge(small_turned, 1)
                    nc.vector.tensor_copy(taps[:, :, 0:TAPS], ps[2][:, 0:CC * 32].rearrange("p (c k) -> p c k", k=32)[:, :, 0:TAPS])
                    nc.vector.tensor_copy(par[:, KC:N_PAR], ps[2][:, T + KC:T + N_PAR]).then_inc(taps_ready, 1)
                    ve.wait_ge(pleT_hi_ready, 1)
                    nc.vector.tensor_tensor(pleT_lo[:, :, :], ps[3][:, :].rearrange("p (k t) -> p k t", k=2),
                                            pleT_hi[:, :, :].bitcast(F32), ALU.subtract).then_inc(pleT_ready, 1)
                if m == 7:
                    mean_square(0, 0)
                mask_steps(m)
                if m == 9:
                    ve.wait_ge(rb_spread, 1)
                    nc.vector.tensor_scalar(q_scale[:, :], rstd[:, 0], SCALE, None, ALU.mult).then_inc(q_scale_ready, 1)
                    nc.vector.tensor_copy(rb[:, :], ps[6][:, 0:T]).then_inc(rb_ready, 1)
                if m == 10:
                    take_panel(0)
                if 8 < m <= WO_A and m % 8 == 0 and IN_PANELS[m // 8 - 1][0] in "ck":
                    take_panel(m // 8 - 1)
                for g in range(2):
                    if m == 16 * (g + 1) + 1:
                        ve.wait_ge(gate_c_ready, g + 1)
                        ve.wait_ge(panel_read, 2 * g + 2)
                        nc.vector.tensor_tensor(u[:, 4 * g:4 * g + 4, PAD:PAD + T], u[:, 4 * g:4 * g + 4, PAD:PAD + T],
                                                gate_c[:, :, :], ALU.mult).then_inc(u_ready, 1)
                for hd in range(HEADS):
                    if m == SCORES_AT[hd]:
                        row_max(hd)
                    if m == SCORES_AT[hd] + 2:
                        normalise(hd)
                    if m == VALUES_AT[hd] + (2 if hd < HEADS - 1 else 1):
                        ve.wait_ge(oT_hi_ready, hd + 1)
                        nc.vector.tensor_tensor(oT_lo[:, hd], values_bank(hd)[:, 0:T], oT_hi[:, hd].bitcast(F32), ALU.subtract).then_inc(oT_ready, 1)
                conv_ops(m)
                ln_steps(m)
                for q, start, halves in ((Q_WO_A, WO_A, 2), (Q_WO_B, WO_B, 2), (Q_WO_C, WO_C, 4)):
                    for c in range(4):
                        if m == start + halves * (c + 1):
                            if q > Q_WO_A:
                                ve.wait_ge(panel_read, q + c - 3)
                            add_panel(q + c, c, m)
                for c in range(4):
                    if m == WO_C + 4 * (c + 1) + 2:
                        gain_lo(1, G_FFN, c, HIGH[0])
                if m == FFN0 + 3:
                    mean_square(1, 2)

            def ln_steps(m):
                def wide(tokens):
                    return tokens.unsqueeze(1).broadcast_to([P, 2, T])
                if m == MEAN_AT:
                    ve.wait_ge(mean_ready, 1)
                    for i in range(4):
                        c = slice(2 * i, 2 * i + 2)
                        nc.vector.tensor_tensor(conv[:, c], conv[:, c], wide(LN_BANK[:, 0:T]), ALU.subtract).then_inc(centered, 1)
                if m == VAR_AT:
                    ve.wait_ge(var_ready, 1)
                    nc.vector.tensor_scalar(msq[:, 4], LN_BANK[:, 0:TT], EPS, None, ALU.add).then_inc(msq_ready, 1)
                if m == SPREAD_AT:
                    ve.wait_ge(ln_spread, 1)
                    ve.wait_ge(centered, 4)
                    for i in range(4):
                        c = slice(2 * i, 2 * i + 2)
                        nc.vector.tensor_tensor(conv[:, c], conv[:, c], wide(LN_BANK[:, 0:T]), ALU.mult).then_inc(ln_scaled, 1)
                if m == SPREAD_AT + 4:
                    for i in range(2):
                        ve.wait_ge(convT_hi_ready, i + 1)
                        nc.vector.tensor_tensor(oT_lo[:, HEADS + 4 * i:HEADS + 4 * i + 4], conv[:, 4 * i:4 * i + 4],
                                                oT_hi[:, HEADS + 4 * i:HEADS + 4 * i + 4].bitcast(F32), ALU.subtract).then_inc(convT_ready, 1)

            def swiglu(j, done):
                ve.wait_ge(half_done, done)
                ve.wait_ge(swish_ready, j + 1)
                for t in range(TT):
                    ins = nc.vector.scalar_tensor_tensor(act[:, t], LOW[1][t][:, :], rstd[:, 1, t:t + 1], swish[:, t], ALU.mult, ALU.mult)
                ins.then_inc(act_ready, 1)

            def act_lo(j):
                ve.wait_ge(actT_hi_ready, j + 1)
                for i in range(2):
                    ins = nc.vector.tensor_tensor(oT_lo[:, 2 * i:2 * i + 2], HIGH[0][i][:, :].rearrange("p (k t) -> p k t", k=2),
                                                  oT_hi[:, 2 * i:2 * i + 2].bitcast(F32), ALU.subtract)
                ins.then_inc(actT_ready, 1)

            for m in range(IN0, LOOP0):
                step(m)
                if not by_pool(m + AHEAD):
                    split_lo(m + AHEAD)
            swiglu(0, LOOP0)
            with ve.Fori(0, LOOPS) as it:
                for t in range(PER_LOOP):
                    if t == 2:
                        act_lo(it)
                    if t == 16:
                        ve.wait_ge(actT_turned, it + 1)
                        swiglu(it + 1, LOOP0 + 16 + PER_LOOP * it)
                    if t in (18, 20, 22):
                        c = (t - 18) // 2
                        ve.wait_ge(panel_read, Q_DOWN + c - 3 + 4 * it)
                        add_panel(Q_DOWN + c, c, LOOP0 + t, it)
                    split_lo(LOOP0 + t + AHEAD, it)
                ve.wait_ge(panel_read, Q_DOWN + 4 * it)
                add_panel(Q_DOWN + 3, 3, LOOP0 + PER_LOOP, it)

            def gate_logits(c, t, cols, bank):
                nc.vector.scalar_tensor_tensor(gate_p[:, t, cols], bank, rstd[:, 2, t:t + 1],
                                               b_rows[:, c * NP + cols.start:c * NP + cols.stop], ALU.mult, ALU.add).then_inc(gate_in, 1)

            def gate_input(c):
                if c:
                    ve.wait_ge(h_ready, c)
                else:
                    ve.wait_ge(rows_loaded, 32)
                    ve.wait_ge(rstd_ready, 4)
                for t in range(TT):
                    gate_logits(c, t, slice(0, NP), pair_of(Q_PG + c)[t][:, :])

            def gated_input(c):
                cols = slice(c * NP, (c + 1) * NP)
                for t in range(TT):
                    ve.wait_ge(gate_p_ready, 2 * c + t + 1)
                    nc.vector.tensor_tensor(gate_p[:, t], gate_p[:, t], pw[:, t, cols], ALU.mult).then_inc(gated, 1)
                for t in range(TT):
                    ve.wait_ge(gated, 2 * c + t + 1)
                    ins = nc.vector.tensor_tensor(h[:, t, cols], h[:, t, cols], gate_p[:, t], ALU.add)
                ins.then_inc(h_ready, 1)

            for m in range(PLE0, END):
                if m == PLE0 + 1:
                    act_lo(LOOPS)
                for c in range(4):
                    if m == DOWN0 + 2 * (c + 1):
                        ve.wait_ge(panel_read, Q_DOWN_LAST + c - 3)
                        add_panel(Q_DOWN_LAST + c, c, m)
                    if m == DOWN0 + 4 + 2 * c:
                        gain_lo(2, G_PLE, c, LOW[0])
                if m == DOWN0 + 11:
                    mean_square(2, 3)
                for c in range(3):
                    if m == PG0 + 8 * (c + 1):
                        ve.wait_ge(half_done, m)
                        gate_input(c)
                    if m == PG0 + 8 * (c + 1) + 1:
                        gated_input(c)
                for i in splits_at(m):
                    split_lo(i)
            def last_gated(i):
                t, cols = LAST_PIECES[i]
                h_cols = slice(3 * NP + cols.start, 3 * NP + cols.stop)
                ve.wait_ge(gate_p_ready, 6 + i + 1)
                nc.vector.tensor_tensor(gate_p[:, t, cols], gate_p[:, t, cols], pw[:, t, h_cols], ALU.mult).then_inc(gated, 1)
                ve.wait_ge(gated, 6 + i + 1)
                nc.vector.tensor_tensor(h[:, t, h_cols], h[:, t, h_cols], gate_p[:, t, cols], ALU.add).then_inc(h_ready, 1)

            def last_gain(i):
                t, cols = LAST_PIECES[i]
                h_cols = slice(3 * NP + cols.start, 3 * NP + cols.stop)
                ve.wait_ge(sq_ready, 8 * 3 + 6 + i + 1)
                nc.vector.tensor_tensor(h[:, t, h_cols], h[:, t, h_cols], gf_rows[:, h_cols], ALU.mult).then_inc(hg_last_ready, 1)

            ve.wait_ge(h_ready, 3)
            for i, (t, cols) in enumerate(LAST_PIECES):
                ve.wait_ge(last_done, i + 1)
                gate_logits(3, t, cols, last_banks[i][:, cols])
                if i == 2:
                    last_gain(1)
                last_gated(i)
                if cols.stop < NP:
                    continue
                ve.wait_ge(sq_ready, 8 * 3 + 6 + i + 1)
                nc.vector.reduce_sum(msq[:, 3, t:t + 1], sq[:, 3, t, 0:4 + t], axis=AX.X).then_inc(sum_ready, 1)
                ve.wait_ge(sum_ready, 3 + t + 1)
                nc.vector.tensor_scalar(msq[:, 3, t:t + 1], msq[:, 3, t:t + 1], 1.0 / D, EPS, ALU.mult, ALU.add).then_inc(msq_ready, 1)
                last_gain(i)
                ve.wait_ge(rstd_ready, 5 + t)
                ve.wait_ge(hg_ready, 6)
                for tile, right, out_cols in OUT_PIECES:
                    if tile == t and not right:
                        nc.vector.tensor_scalar(h[:, t, out_cols], h[:, t, out_cols], rstd[:, 3, t:t + 1], None, ALU.mult).then_inc(y_left_ready, 1)

        @block.tensor
        def _(pe):
            def arrived(m, it=0):
                pe.wait_ge(lo_ready_pool if by_pool(m) else lo_ready, lo_count(m, it))

            def tokens_by_columns(m, banks, x_hi, x_lo, first, last, it=0):
                arrived(m, it)
                s = m % SLOTS
                for k in range(2):
                    for t in range(TT):
                        rows = slice(t * P, (t + 1) * P)
                        start, stop = first and k == 0, last and k == 1
                        nc.tensor.matmul(banks[t][:, :], x_hi[:, k, rows], w_hi[:, s, k], start=start, stop=False)
                        nc.tensor.matmul(banks[t][:, :], x_hi[:, k, rows], w_lo[:, s, k], start=False, stop=False)
                        ins = nc.tensor.matmul(banks[t][:, :], x_lo[:, k, rows], w_hi[:, s, k], start=False, stop=stop)
                ins.then_inc(half_done, 1)

            def columns_by_tokens(m, banks, x_hi, x_lo, first, last):
                arrived(m)
                s = m % SLOTS
                for k in range(2):
                    for c in range(4):
                        dst = banks[c // 2][:, (c % 2) * T:(c % 2 + 1) * T]
                        cols = slice(c * P, (c + 1) * P)
                        start, stop = first and k == 0 and c % 2 == 0, last and k == 1
                        nc.tensor.matmul(dst, w_hi[:, s, k, cols], x_hi[:, k], start=start, stop=False, skip_group_check=True)
                        nc.tensor.matmul(dst, w_hi[:, s, k, cols], x_lo[:, k], start=False, stop=False, skip_group_check=True)
                        ins = nc.tensor.matmul(dst, w_lo[:, s, k, cols], x_hi[:, k], start=False, stop=stop, skip_group_check=True)
                ins.then_inc(half_done, 1)

            def turn(src, c, banks, chunks=range(4)):
                for k in chunks:
                    for t in range(TT):
                        at = (k % 2) * T + t * P
                        ins = nc.tensor.transpose(banks[k // 2][:, at:at + P], src[:, t, c * NP + k * P:c * NP + (k + 1) * P], ident[:, :])
                return ins

            def turn_h(norm, c, banks):
                turn(h, c, banks).then_inc(hT_done, 1)

            def scores(hd):
                g, i = hd // 4, hd % 4
                pe.wait_ge(panel_read, (6, 9)[g])
                if hd:
                    pe.wait_ge(masked_ready, hd)
                else:
                    pe.wait_ge(conv_step, CONV_OPS)
                bank = SCORES_BANK
                nc.tensor.matmul(bank[:, 0:P], qT[:, i, 0:P], kT[:, i, 0:P], start=True, stop=True)
                nc.tensor.matmul(bank[:, P:384], qT[:, i, P:T], kT[:, i, 0:T], start=True, stop=True).then_inc(scores_ready, 1)

            def turn_probs(hd):
                pe.wait_ge(prob_ready, hd + 1)
                if hd:
                    pe.wait_ge(probT_ready, hd)
                for b in range(3):
                    ins = nc.tensor.transpose(ps[6][:, b * P:(b + 1) * P], prob[:, hd % 2, b * P:(b + 1) * P], ident[:, :])
                ins.then_inc(probT_turned, 1)

            def values(hd):
                g, b = hd // 4, hd % 4
                pe.wait_ge(panel_read, (7, 10)[g])
                pe.wait_ge(probT_ready, hd + 1)
                if hd in (5, 7):
                    pe.wait_ge(masked_ready, HEADS)
                if hd:
                    pe.wait_ge(oT_ready, hd if hd <= 4 else hd - 1)
                bank = values_bank(hd)
                cols = slice(hd * DH, (hd + 1) * DH)
                nc.tensor.matmul(bank[:, 0:P], v_sb[:, 0, cols], probT[:, b, 0:P], start=True, stop=True)
                nc.tensor.matmul(bank[:, P:T], v_sb[:, 0, cols], probT[:, b, P:2 * P], start=True, stop=False)
                nc.tensor.matmul(bank[:, P:T], v_sb[:, 1, cols], probT[:, b, 2 * P:3 * P], start=False, stop=True).then_inc(o_done, 1)

            def spread(norm, bank, at):
                for t in range(TT):
                    ins = nc.tensor.matmul(bank[:, at + t * P:at + (t + 1) * P], rstd[:, norm, t:t + 1].broadcast_to([P, P]),
                                           ident[:, :], start=True, stop=True)
                return ins

            def before(m):
                if m == 0:
                    warm_up(WARM_UPS[1])
                    pe.wait_ge(x_first, 16)
                    turn(h, 0, HIGH[0], range(2)).then_inc(hT_first, 1)
                    pe.wait_ge(x_loaded[0], 16)
                    turn(h, 0, HIGH[0], range(2, 4)).then_inc(hT_done, 1)
                    warm_up(WARM_UPS[2])
                    pe.wait_ge(nT_first, 1)
                if m == 1:
                    pe.wait_ge(nT_ready, 1)
                for c in {1: (1,), 2: (2,), 4: (3,)}.get(m, ()):
                    pe.wait_ge(x_loaded[c], 16)
                    if c >= 2:
                        pe.wait_ge(nT_ready, c - 1)
                    turn_h(0, c, HIGH[c % 2])
                if m == 6:
                    pe.wait_ge(small_loaded, 16 * 7)
                    pe.wait_ge(par_ready, 1)
                    for c in range(CC):
                        nc.tensor.transpose(ps[2][:, c * 32:c * 32 + TAPS], taps_raw[0:TAPS, c * P:(c + 1) * P], ident[0:TAPS, 0:TAPS])
                    nc.tensor.transpose(ps[2][:, T:T + N_PAR], par_raw[0:N_PAR, :], ident[0:N_PAR, 0:N_PAR])
                    for k in range(2):
                        for t in range(TT):
                            at = k * T + t * P
                            ins = nc.tensor.transpose(ps[3][:, at:at + P], p_raw[:, t, k * P:(k + 1) * P], ident[:, :])
                    ins.then_inc(small_turned, 1)
                if 2 <= m < 8 and m % 2 == 0:
                    pe.wait_ge(nT_ready, m // 2 + 1)
                if m == 9:
                    pe.wait_ge(rstd_ready, 1)
                    spread(0, ps[6], 0).then_inc(rb_spread, 1)
                if m == 10:
                    pe.wait_ge(rb_ready, 1)
                if m == 8:
                    pe.wait_ge(taps_ready, 1)
                    pe.wait_ge(pleT_ready, 1)
                for hd in range(HEADS):
                    if m == SCORES_AT[hd]:
                        scores(hd)
                    if m == TURN_AT[hd]:
                        turn_probs(hd)
                    if m == VALUES_AT[hd]:
                        values(hd)
                if m == MEAN_AT:
                    pe.wait_ge(consts_ready, 1)
                    pe.wait_ge(conv_added, 4)
                    for g in range(2):
                        ins = nc.tensor.matmul(LN_BANK[:, 0:T], mean_w[:, :], group_sum[:, g], start=g == 0, stop=g == 1)
                    ins.then_inc(mean_ready, 1)
                if m == VAR_AT:
                    pe.wait_ge(dev_added, 3)
                    for t in range(TT):
                        for c in range(2):
                            ins = nc.tensor.matmul(LN_BANK[:, t:t + 1], u[:, c, t * P:(t + 1) * P], mean_w[:, 0:1],
                                                   start=c == 0, stop=c == 1)
                    ins.then_inc(var_ready, 1)
                if m == SPREAD_AT:
                    pe.wait_ge(rstd_ready, 2)
                    spread(4, LN_BANK, 0).then_inc(ln_spread, 1)
                if m == WO_A:
                    pe.wait_ge(oT_ready, 4)
                if m in (WO_C, WO_C + 2):
                    pe.wait_ge(convT_ready, (m - WO_C) // 2 + 1)
                if m == WO_B:
                    pe.wait_ge(oT_ready, HEADS)
                for c in range(4):
                    if m == WO_C + 4 * (c + 1) + 2:
                        pe.wait_ge(panel_read, Q_WO_C + c + 1)
                        pe.wait_ge(nT_ready, 4 + c)
                        turn_h(1, c, HIGH[0])
                    if m == FFN0 + 2 * c:
                        pe.wait_ge(nT_ready, 4 + c + 1)

            def turn_last(c):
                pe.wait_ge(panel_read, Q_DOWN_LAST + c + 1)
                if c:
                    pe.wait_ge(nT_ready, 8 + c)
                else:
                    pe.wait_ge(pw_ready, 4)
                turn_h(2, c, LOW[0])

            def turn_act(j):
                pe.wait_ge(act_ready, j + 1)
                pe.wait_ge(panel_read, Q_DOWN - 1 + 4 * j)
                turn(act, 0, HIGH[0]).then_inc(actT_turned, 1)

            def warm_up(times):
                for _ in range(times):
                    nc.tensor.matmul(ps[7][:, 0:P], mean_w[:, :], mean_w[:, :], start=True, stop=True)

            pe.wait_ge(consts_ready, 1)
            warm_up(WARM_UPS[0])
            pe.wait_ge(ident_ready, 2)
            pe.wait_ge(par_loaded, 16)
            nc.tensor.transpose(ps[3][:, 0:KC], par_raw[0:KC, :], ident[0:KC, 0:KC]).then_inc(par_turned, 1)
            for m in range(IN0, WO_A):
                before(m)
                q, k = m // 8, m % 8
                if k == 0 and q >= 2:
                    pe.wait_ge(panel_read, q - 1)
                product = tokens_by_columns if IN_PANELS[q][0] == "v" else columns_by_tokens
                rows = slice(2 * k, 2 * k + 2)
                product(m, pair_of(q), nT_hi[:, rows], nT_lo[:, rows], k == 0, k == 7)
            for q0, start, halves, k0 in ((Q_WO_A, WO_A, 2, 0), (Q_WO_B, WO_B, 2, 4), (Q_WO_C, WO_C, 4, HEADS)):
                for c in range(4):
                    for k in range(halves):
                        m = start + halves * c + k
                        before(m)
                        if k == 0:
                            pe.wait_ge(panel_read, q0 + c - 1)
                        rows = slice(k0 + 2 * k, k0 + 2 * k + 2)
                        tokens_by_columns(m, pair_of(q0 + c), oT_hi[:, rows], oT_lo[:, rows], k == 0, k == halves - 1)
            for m in range(FFN0, LOOP0):
                before(m)
                k = m % 8
                if k == 0:
                    pe.wait_ge(panel_read, Q_DOWN - 1 if m == FFN0 else Q_DOWN)
                rows = slice(2 * k, 2 * k + 2)
                tokens_by_columns(m, LOW[(m - FFN0) // 8], nT_hi[:, rows], nT_lo[:, rows], k == 0, k == 7)
            with pe.Fori(0, LOOPS) as it:
                pe.wait_ge(swish_ready, it + 1)
                for k in range(8):
                    if k == 2:
                        turn_act(it)
                    rows = slice(2 * k, 2 * k + 2)
                    tokens_by_columns(LOOP0 + k, LOW[0], nT_hi[:, rows], nT_lo[:, rows], k == 0, k == 7, it)
                pe.wait_ge(act_ready, it + 1)
                for k in range(8):
                    rows = slice(2 * k, 2 * k + 2)
                    tokens_by_columns(LOOP0 + 8 + k, LOW[1], nT_hi[:, rows], nT_lo[:, rows], k == 0, k == 7, it)
                pe.wait_ge(actT_ready, it + 1)
                for c in range(4):
                    pe.wait_ge(panel_read, Q_DOWN + c - 1 + 4 * it)
                    for k in range(2):
                        rows = slice(2 * k, 2 * k + 2)
                        tokens_by_columns(LOOP0 + 16 + 2 * c + k, pair_of(Q_DOWN + c), oT_hi[:, rows], oT_lo[:, rows], k == 0, k == 1, it)
            for c in range(2):
                if c == 0:
                    pe.wait_ge(swish_ready, FP)
                    turn_act(LOOPS)
                else:
                    pe.wait_ge(panel_read, Q_DOWN_LAST)
                for k in range(2):
                    m = PLE0 + 2 * c + k
                    arrived(m)
                    for f in range(2):
                        if c == 1 and k == 0 and f == 1:
                            pe.wait_ge(pw_ready, 1)
                        for t in range(TT):
                            rows = slice(t * P, (t + 1) * P)
                            dst = PLE_BANKS[2 * c + f][t][:, :]
                            nc.tensor.matmul(dst, pleT_hi[:, k, rows], w_hi[:, m % SLOTS, f], start=k == 0, stop=False)
                            nc.tensor.matmul(dst, pleT_hi[:, k, rows], w_lo[:, m % SLOTS, f], start=False, stop=False)
                            ins = nc.tensor.matmul(dst, pleT_lo[:, k, rows], w_hi[:, m % SLOTS, f], start=False, stop=k == 1)
                    ins.then_inc(half_done, 1)
            pe.wait_ge(actT_ready, FP)
            for c in range(4):
                pe.wait_ge(panel_read, Q_DOWN_LAST + c - 1)
                if c == 1:
                    pe.wait_ge(pw_ready, 3)
                for k in range(2):
                    if k == 0 and c >= 2:
                        turn_last(c - 2)
                    rows = slice(2 * k, 2 * k + 2)
                    tokens_by_columns(DOWN0 + 2 * c + k, pair_of(Q_DOWN_LAST + c), oT_hi[:, rows], oT_lo[:, rows], k == 0, k == 1)
            for c in range(3):
                if c < 2:
                    pe.wait_ge(panel_read, Q_PG + c - 1)
                else:
                    pe.wait_ge(gate_in, 2 * (c - 1))
                for k in range(8):
                    if c == 0 and k in (0, 2):
                        turn_last(2 + k // 2)
                    if c == 0 and k % 2 == 0:
                        pe.wait_ge(nT_ready, 8 + k // 2 + 1)
                    rows = slice(2 * k, 2 * k + 2)
                    tokens_by_columns(PG0 + 8 * c + k, pair_of(Q_PG + c), nT_hi[:, rows], nT_lo[:, rows], k == 0, k == 7)
            pe.wait_ge(gate_in, 4)
            for i, (t, cols) in enumerate(LAST_PIECES):
                for m in range(LAST, END):
                    if i == 0:
                        arrived(m)
                    hi, lo = slot_of(m)
                    for k in range(2):
                        row = 2 * (m - LAST) + k
                        dst, tok = last_banks[i][:, cols], slice(t * P, (t + 1) * P)
                        nc.tensor.matmul(dst, nT_hi[:, row, tok], hi[:, k, cols], start=row == 0, stop=False)
                        nc.tensor.matmul(dst, nT_hi[:, row, tok], lo[:, k, cols], start=False, stop=False)
                        ins = nc.tensor.matmul(dst, nT_lo[:, row, tok], hi[:, k, cols], start=False, stop=row == KC - 1)
                ins.then_inc(last_done, 1)


_INS = ["x", "p", "g_mix", "w_in", "w_dw", "b_dw", "g_conv_ln", "b_conv_ln", "w_out", "g_ffn",
        "w_gate", "w_up", "w_down", "g_ple", "w_pgate", "b_pgate", "w_ple", "g_final"]


def kernel(**inputs):
    import numpy as np
    import concourse.bacc as bacc
    from concourse.bass_utils import run_bass_kernel_spmd

    nc = bacc.Bacc("TRN2", target_bir_lowering=False, num_devices=1)
    arrays, args = {}, []
    for name in _INS:
        a = np.ascontiguousarray(inputs[name])
        arrays[f"in_{name}"] = a
        args.append(nc.dram_tensor(f"in_{name}", a.shape, mybir.dt.from_np(a.dtype), kind="ExternalInput").ap())
    out = nc.dram_tensor("out", (1, T, D), F32, kind="ExternalOutput").ap()
    hybrid_decoder_layer(nc, *args, out)
    r = run_bass_kernel_spmd(nc, [arrays], core_ids=[0])
    return r.results[0]["out"]
```
